# Optimizing a Trainium2 kernel written in Bass

```python
import math
import jax, jax.numpy as jnp
from jax import lax
import numpy as np

D_MODEL = 1024
BATCH = 1
SEQ = 1024
DEPTH = 1

GRID_W = 64
CONV_W = 512
CONV_K = 3
N_HEADS = 8
HEAD_DIM = 64
ATTN_W = N_HEADS * HEAD_DIM
WIN_R = 8
WIN_C = 16
Q_ROWS = 8
Q_COLS = 16
K_COLS = 32
N_CBLK = GRID_W // Q_COLS
NEG_INF = -1e30
N_BRANCH = 2
PROJ_W = 3 * CONV_W + 3 * ATTN_W + N_BRANCH * D_MODEL
N_EXPERTS = 32
TOP_K = 4
D_EXPERT = D_MODEL
SWIGLU_ALPHA = 1.702
SWIGLU_LIMIT = 7.0
MOE_BLOCK = 128
NORM_EPS = 1e-6

kernel_name = "hybrid_shortconv_natten_moe_block"

def rms_norm(x, g):
    xf = x.astype(jnp.float32)
    y = xf * lax.rsqrt(jnp.mean(xf * xf, axis=-1, keepdims=True) + NORM_EPS)
    return (y * g.astype(jnp.float32)).astype(x.dtype)

def short_conv_mixer(x_in, b_gate, c_gate, conv_w):
    u = c_gate * x_in
    up = jnp.pad(u, ((0, 0), (1, 1), (0, 0)))
    conv = conv_w[0] * up[:, :-2] + conv_w[1] * up[:, 1:-1] + conv_w[2] * up[:, 2:]
    return b_gate * conv

def grid_layout(rows):
    wr = min(WIN_R, rows)
    qr = math.gcd(rows, Q_ROWS)
    kr = min(rows, qr + wr)
    n_rb = rows // qr
    rs = np.clip(np.arange(rows) - wr // 2, 0, rows - wr)
    cs = np.clip(np.arange(GRID_W) - WIN_C // 2, 0, GRID_W - WIN_C)
    q_rows = np.arange(rows).reshape(n_rb, qr)
    q_cols = np.arange(GRID_W).reshape(N_CBLK, Q_COLS)
    key_rows = np.clip(q_rows[:, 0] - wr // 2, 0, rows - kr)[:, None] + np.arange(kr)
    key_cols = np.clip(q_cols[:, 0] - WIN_C // 2, 0, GRID_W - K_COLS)[:, None] + np.arange(K_COLS)
    kr_b = key_rows[:, None, None, None, :, None]
    qr_b = q_rows[:, None, :, None, None, None]
    kc_b = key_cols[None, :, None, None, None, :]
    qc_b = q_cols[None, :, None, :, None, None]
    valid = ((kr_b >= rs[qr_b]) & (kr_b < rs[qr_b] + wr)
             & (kc_b >= cs[qc_b]) & (kc_b < cs[qc_b] + WIN_C))
    ridx = np.clip(kr_b - qr_b + WIN_R - 1, 0, 2 * WIN_R - 2)
    cidx = np.clip(kc_b - qc_b + WIN_C - 1, 0, 2 * WIN_C - 2)
    return qr, key_rows, key_cols, valid, ridx, cidx

def neighbourhood_attention(q, k, v, rpb):
    b, s, h, hd = q.shape
    rows = s // GRID_W
    qr, key_rows, key_cols, valid, ridx, cidx = grid_layout(rows)
    n_rb = rows // qr
    qg = q.reshape(b, n_rb, qr, N_CBLK, Q_COLS, h, hd)
    ridx_g = key_rows[:, :, None, None]
    cidx_g = key_cols[None, None, :, :]
    kg = k.reshape(b, rows, GRID_W, h, hd)[:, ridx_g, cidx_g]
    vg = v.reshape(b, rows, GRID_W, h, hd)[:, ridx_g, cidx_g]
    bias = jnp.where(jnp.asarray(valid), rpb[:, ridx, cidx].astype(jnp.float32), NEG_INF)
    scores = jnp.einsum('biajchd,bikjlhd->bhijackl', qg, kg,
                        preferred_element_type=jnp.float32) * (HEAD_DIM ** -0.5) + bias[None]
    probs = jax.nn.softmax(scores.reshape(*scores.shape[:-2], -1), axis=-1).reshape(scores.shape)
    out = jnp.einsum('bhijackl,bikjlhd->biajchd', probs.astype(v.dtype), vg)
    return out.reshape(b, s, h * hd)

def moe_ffn(h, w_router, b_router, w_gate, b_gate, w_up, b_up, w_down, b_down):
    b, s, d = h.shape
    n_tok = b * s
    n_asg = n_tok * TOP_K
    xt = h.reshape(n_tok, d)
    logits = jnp.dot(xt, w_router, preferred_element_type=jnp.float32) + b_router.astype(jnp.float32)
    top_v, top_i = lax.top_k(logits, TOP_K)
    gates = jax.nn.softmax(top_v, axis=-1)
    e_flat = top_i.reshape(n_asg).astype(jnp.int32)
    tok_flat = jnp.arange(n_asg, dtype=jnp.int32) // TOP_K
    order = jnp.argsort(e_flat)
    e_sorted = e_flat[order]
    tok_sorted = tok_flat[order]
    g_sorted = gates.reshape(n_asg)[order]
    counts = jnp.zeros((N_EXPERTS,), jnp.int32).at[e_flat].add(1)
    group_start = jnp.cumsum(counts) - counts
    padded = (counts + MOE_BLOCK - 1) // MOE_BLOCK * MOE_BLOCK
    padded_end = jnp.cumsum(padded)
    padded_start = padded_end - padded
    dest = padded_start[e_sorted] + jnp.arange(n_asg, dtype=jnp.int32) - group_start[e_sorted]
    n_blocks = -(-n_asg // MOE_BLOCK) + N_EXPERTS
    n_rows = n_blocks * MOE_BLOCK
    row_token = jnp.zeros((n_rows,), jnp.int32).at[dest].set(tok_sorted)
    row_gate = jnp.zeros((n_rows,), jnp.float32).at[dest].set(g_sorted)
    block_expert = jnp.minimum(
        jnp.searchsorted(padded_end, jnp.arange(n_blocks, dtype=jnp.int32) * MOE_BLOCK, side='right'),
        N_EXPERTS - 1).astype(jnp.int32)

    def expert_block(args):
        idx, gate, e = args
        xb = xt[idx]
        g = jnp.minimum(xb @ w_gate[e] + b_gate[e], SWIGLU_LIMIT)
        u = jnp.clip(xb @ w_up[e] + b_up[e], -SWIGLU_LIMIT, SWIGLU_LIMIT)
        act = g * jax.nn.sigmoid(SWIGLU_ALPHA * g) * (u + 1)
        y = act @ w_down[e] + b_down[e]
        return y * gate[:, None].astype(y.dtype)

    y_rows = lax.map(expert_block, (row_token.reshape(n_blocks, MOE_BLOCK),
                                    row_gate.reshape(n_blocks, MOE_BLOCK),
                                    block_expert)).reshape(n_rows, d)
    y = jax.ops.segment_sum(y_rows, row_token, num_segments=n_tok)
    return y.reshape(b, s, d).astype(h.dtype)

def setup_inputs(seed: int = 0) -> dict:
    key = jax.random.key(seed)
    ks = jax.random.split(key, 20)
    f32 = jnp.float32
    nrm = lambda k, shape, scale: jax.random.normal(k, shape, f32) * scale
    L, D, E, F = DEPTH, D_MODEL, N_EXPERTS, D_EXPERT
    return {
        'x': nrm(ks[0], (BATCH, SEQ, D), 1.0),
        'norm_mix': 1.0 + nrm(ks[1], (L, D), 0.01),
        'w_in': nrm(ks[2], (L, D, PROJ_W), D ** -0.5),
        'conv_w': nrm(ks[3], (L, CONV_K, CONV_W), CONV_K ** -0.5),
        'w_out_conv': nrm(ks[4], (L, CONV_W, D), CONV_W ** -0.5),
        'q_norm': 1.0 + nrm(ks[5], (L, HEAD_DIM), 0.01),
        'k_norm': 1.0 + nrm(ks[6], (L, HEAD_DIM), 0.01),
        'rpb': nrm(ks[7], (L, N_HEADS, 2 * WIN_R - 1, 2 * WIN_C - 1), 0.02),
        'w_out_attn': nrm(ks[8], (L, ATTN_W, D), ATTN_W ** -0.5),
        'w_o': nrm(ks[9], (L, D, D), D ** -0.5),
        'norm_ffn': 1.0 + nrm(ks[10], (L, D), 0.01),
        'w_router': nrm(ks[11], (L, D, E), D ** -0.5),
        'b_router': nrm(ks[12], (L, E), 0.01),
        'w_gate': nrm(ks[13], (L, E, D, F), D ** -0.5),
        'b_gate': nrm(ks[14], (L, E, F), 0.01),
        'w_up': nrm(ks[15], (L, E, D, F), D ** -0.5),
        'b_up': nrm(ks[16], (L, E, F), 0.01),
        'w_down': nrm(ks[17], (L, E, F, D), F ** -0.5),
        'b_down': nrm(ks[18], (L, E, D), 0.01),
    }

def reference(x, norm_mix, w_in, conv_w, w_out_conv, q_norm, k_norm, rpb, w_out_attn, w_o,
              norm_ffn, w_router, b_router, w_gate, b_gate, w_up, b_up, w_down, b_down):
    b, s, d = x.shape
    split_points = [CONV_W, 2 * CONV_W, 3 * CONV_W,
                    3 * CONV_W + ATTN_W, 3 * CONV_W + 2 * ATTN_W, 3 * CONV_W + 3 * ATTN_W,
                    3 * CONV_W + 3 * ATTN_W + D_MODEL]
    for l in range(DEPTH):
        h = rms_norm(x, norm_mix[l])
        proj = h @ w_in[l]
        x_in, b_g, c_g, q, k, v, gate_a, gate_b = jnp.split(proj, split_points, axis=-1)
        y_conv = short_conv_mixer(x_in, b_g, c_g, conv_w[l]) @ w_out_conv[l]
        q = rms_norm(q.reshape(b, s, N_HEADS, HEAD_DIM), q_norm[l])
        k = rms_norm(k.reshape(b, s, N_HEADS, HEAD_DIM), k_norm[l])
        v = v.reshape(b, s, N_HEADS, HEAD_DIM)
        y_attn = neighbourhood_attention(q, k, v, rpb[l]) @ w_out_attn[l]
        mixed = jax.nn.sigmoid(gate_a) * y_conv + jax.nn.sigmoid(gate_b) * y_attn
        x = x + mixed @ w_o[l]
        h = rms_norm(x, norm_ffn[l])
        x = x + moe_ffn(h, w_router[l], b_router[l], w_gate[l], b_gate[l],
                        w_up[l], b_up[l], w_down[l], b_down[l])
    return x


_drawn_inputs = setup_inputs


def setup_inputs(seed=0):
    import zlib

    import numpy as np

    out = dict(_drawn_inputs(seed))
    spreads = {}
    factors = {'q_norm': 7.264,
     'k_norm': 8.0,
     'rpb': 17.458,
     'b_gate': 8.0,
     'b_up': 21.606,
     'b_down': 8.0}
    for name, (base, spread) in spreads.items():
        noise = np.random.default_rng([zlib.crc32(name.encode()), seed]).standard_normal(out[name].shape)
        drawn = base * np.exp(spread * noise) if base else spread * noise
        out[name] = __import__('jax').numpy.asarray(drawn.astype(out[name].dtype))
    for name, factor in factors.items():
        out[name] = (out[name] * factor).astype(out[name].dtype)
    return out
```

```python
from contextlib import ExitStack

import numpy as np
import concourse.bass as bass
from concourse import mybir

F32 = mybir.dt.float32
BF16 = mybir.dt.bfloat16
I32 = mybir.dt.int32
U32 = mybir.dt.uint32
ALU = mybir.AluOpType
ACT = mybir.ActivationFunctionType
AX = mybir.AxisListType

P = 128
D = 1024
S = 1024
KT = D // P
TT = S // P
CONV = 512
HEADS, HD = 8, 64
GRID_W, ROWS = 64, S // 64
WIN_R, WIN_C = 8, 16
QR, QC = 8, 16
KR, KC = 12, 32
KEYS = KR * KC
ROW_BASE = [0, 4]
COL_BASE = [0, 8, 24, 32]
COL_VAR = [0, 1, 1, 2]
BIG = 1e30
E, TOPK = 32, 4
SLOTS = 2 * P
MAX_PASSES = E + S * TOPK // SLOTS
NT = MAX_PASSES + 2
DUMMY = S
ROWS_OUT = S + SLOTS
EPS = 1e-6
LIMIT, ALPHA = 7.0, 1.702
FQ = 256
STEPS = 6
CH = 2048
NSLOT = 6
MSLOT = 4
WIN = 15 * 63 + 48


def layout(np_inputs):
    a = {k: np.asarray(v) for k, v in np_inputs.items()}
    cols = lambda v: np.ascontiguousarray(v.reshape(-1, P).T)
    pad = np.zeros((HEADS, 23, 63), np.float32)
    pad[:, 4:19, 16:47] = a["rpb"][0]
    flat = pad.reshape(HEADS, -1)
    q = np.arange(P)
    start = (7 - q // QC) * 63 + 15 - q % QC
    windows = flat[:, start[:, None] + np.arange(WIN)[None, :]]
    return {
        "x": a["x"][0], "nmix": cols(a["norm_mix"][0]), "w_in": a["w_in"][0],
        "convw": np.ascontiguousarray(a["conv_w"][0].reshape(3, 4, P).transpose(2, 0, 1).reshape(P, 12)),
        "w_oc": a["w_out_conv"][0],
        "qkgain": np.stack([np.tile(a["k_norm"][0], 2), np.tile(a["q_norm"][0], 2)], 1),
        "windows": np.ascontiguousarray(windows), "w_oa": a["w_out_attn"][0], "w_o": a["w_o"][0],
        "nffn": cols(a["norm_ffn"][0]), "w_r": a["w_router"][0], "b_r": a["b_router"],
        "w_gate": a["w_gate"][0], "b_gate": a["b_gate"][0], "w_up": a["w_up"][0], "b_up": a["b_up"][0],
        "w_down": a["w_down"][0], "b_down": a["b_down"][0],
    }


def window_masks():
    out = np.zeros((P, 2, 3, KR, KC), np.float32)
    q = np.arange(P)
    for rb in range(2):
        r = 8 * rb + q // QC
        rs = np.clip(r - WIN_R // 2, 0, ROWS - WIN_R)
        kr = ROW_BASE[rb] + np.arange(KR)
        row_ok = (kr[None] >= rs[:, None]) & (kr[None] < rs[:, None] + WIN_R)
        for cb in (0, 1, 3):
            c = QC * cb + q % QC
            cs = np.clip(c - WIN_C // 2, 0, GRID_W - WIN_C)
            kc = COL_BASE[cb] + np.arange(KC)
            col_ok = (kc[None] >= cs[:, None]) & (kc[None] < cs[:, None] + WIN_C)
            ok = row_ok[:, :, None] & col_ok[:, None, :]
            out[:, rb, COL_VAR[cb]] = np.where(ok, 0.0, BIG)
    return out.reshape(P, 6 * KEYS)


def build(nc, A, out):
    ctx = ExitStack()
    with ctx:
        def sem(name):
            return ctx.enter_context(nc.semaphore(name))

        def sb(name, shape, dt=F32, where=ctx):
            return where.enter_context(nc.sbuf_tensor(name, shape, dt))

        bank = [ctx.enter_context(nc.psum_tensor(f"bank{i}", [P, 512], F32)) for i in range(8)]
        h2_rows = nc.dram_tensor("h2_rows", [ROWS_OUT, D], F32).ap()

        ring = sb("ring", [P, NSLOT, CH])
        ident = sb("ident", [P, P])
        ones_bf = sb("ones_bf", [P, P], BF16)
        tri_bf = sb("tri_bf", [P, P], BF16)
        ones_row = sb("ones_row", [1, P])
        br_row = sb("br_row", [1, E])
        wr = sb("wr", [P, KT, E])
        nmix = sb("nmix", [P, KT])
        nffn = sb("nffn", [P, KT])
        convw = sb("convw", [P, 12])
        gain = sb("gain", [P, 2])
        ss = sb("ss", [P, TT])
        var = sb("var", [P, TT])
        rstd = sb("rstd", [P, TT])
        half = sb("half", [P, 8])
        logits = sb("logits", [P, TT, E])
        top_v = sb("top_v", [P, TT, 8])
        top_i = sb("top_i", [P, TT, 8], U32)
        iota_i = sb("iota_i", [P, SLOTS], I32)
        iota_f = sb("iota_f", [P, SLOTS])
        ctile_i = sb("ctile_i", [P, TT * E], I32)
        cpart_i = sb("cpart_i", [P, TT * E], I32)
        dum_i = sb("dum_i", [P, 2], I32)
        dum = sb("dum", [P, 2])
        rows_bf = sb("rows_bf", [P, TT, E, 6], BF16)
        slot_of = sb("slot_of", [P, TT, E])
        table = sb("table", [1, 3 * NT + 1], I32)

        mix = ExitStack()
        hT = sb("hT", [P, KT, S], where=mix)
        qkT = sb("qkT", [P, 8, S], where=mix)
        vb = sb("vb", [P, 4, 4, CONV], where=mix)
        ypre = sb("ypre", [P, 4, S], where=mix)
        oT = sb("oT", [P, 4, S], where=mix)
        masks = sb("masks", [P, 6, KEYS], BF16, where=mix)
        bias = sb("bias", [P, 6, KEYS], where=mix)
        win = sb("win", [P, 16, 63], where=mix)
        ra, rb_ = ring[:, MSLOT, :], ring[:, MSLOT + 1, :]
        ss8 = sb("ss8", [P, 2, 8], where=mix)
        var8 = sb("var8", [P, 2, 8], where=mix)
        rs8 = sb("rs8", [P, 2, 8], where=mix)
        nmin = sb("nmin", [P, 2], where=mix)
        rsum = sb("rsum", [P, 2], where=mix)
        rinv = sb("rinv", [P, 2], where=mix)
        mixedT = qkT
        vnat = oT[:, :, :].rearrange("p a (b n) -> p (a b) n", b=2)
        xt = [ra[:, 0:1024], ra[:, 1024:2048]]
        junk = rb_[:, 0:1024]
        sq = rb_[:, 0:512]
        qn = [rb_[:, 512:1024], rb_[:, 1024:1536]]
        prob = [rb_[:, 0:384], rb_[:, 384:768]]
        probT = [rb_[:, 768:1152], rb_[:, 1152:1536]]
        u = [ra[:, 0:1024], ra[:, 1024:2048]]
        tmp = [ra[:, 512 * i:512 * i + 512] for i in range(4)]
        xe = [rb_[:, 0:1024], rb_[:, 1024:2048]]
        xn = [ra[:, 0:1024], ra[:, 1024:2048]]
        h2T = [hT[:, 0, :].rearrange("p (k t) -> p k t", k=KT), hT[:, 1, :].rearrange("p (k t) -> p k t", k=KT)]
        junk_e = hT[:, 2, :]
        mix.close()

        moe = ExitStack()
        rt = sb("rt", [P, 5, TT * E], where=moe)
        oh = sb("oh", [P, TT * TOPK, E], where=moe)
        ohg = sb("ohg", [P, TT * TOPK, E], where=moe)
        topi_f = sb("topi_f", [P, TT, TOPK], where=moe)
        ev = sb("ev", [P, TT, TOPK], where=moe)
        gk = sb("gk", [P, TT, TOPK], where=moe)
        esum = sb("esum", [P, TT], where=moe)
        routed_bf = sb("routed_bf", [P, TT * E], BF16, where=moe)
        before = sb("before", [P, TT + 1, E], where=moe)
        npass = sb("npass", [P, E], where=moe)
        scan = sb("scan", [P, 2, 16 + E], where=moe)
        pexc = sb("pexc", [P, E], where=moe)
        big1 = sb("big1", [1, NT, E], where=moe)
        big2 = sb("big2", [1, NT, E], where=moe)
        row1 = sb("row1", [1, 6, NT], where=moe)
        scanb = sb("scanb", [1, 2, 64 + NT], where=moe)
        xg = [sb(f"xg{b}", [P, D], where=moe) for b in range(2)]
        xT = [sb(f"xT{b}", [P, KT, P], where=moe) for b in range(2)]
        aT = [sb(f"aT{b}", [P, KT, P], where=moe) for b in range(2)]
        gu = [sb(f"gu{b}", [P, 2 * FQ], where=moe) for b in range(2)]
        sg = [sb(f"sg{b}", [P, FQ], where=moe) for b in range(2)]
        act = [sb(f"act{b}", [P, FQ], where=moe) for b in range(2)]
        yt = [sb(f"yt{b}", [P, 512], where=moe) for b in range(2)]
        ys = [sb(f"ys{b}", [P, D], where=moe) for b in range(2)]
        brow = sb("brow", [1, 3 * D], where=moe)
        bbc = sb("bbc", [P, 3 * D], where=moe)
        pick = sb("pick", [P, TT, SLOTS], BF16, where=moe)
        slot_col = sb("slot_col", [P, TT, 1], where=moe)
        islot = sb("islot", [P, 12], where=moe)
        itmp = sb("itmp", [P, 3, 2], where=moe)
        idx_next = sb("idx_next", [P, 2], U32, where=moe)
        idx_cur = sb("idx_cur", [P, 2], U32, where=moe)
        gate_next = sb("gate_next", [P, 2], where=moe)
        gate_cur = sb("gate_cur", [P, 2], where=moe)
        gsum = sb("gsum", [P, 2], where=moe)
        moe.close()

        consts_in = sem("consts_in")
        made = sem("made")
        pool_c = sem("pool_c")
        zero_out = sem("zero_out")
        x_in = [sem(f"x_in{i}") for i in range(2)]
        w_in = [sem(f"w_in{i}") for i in range(MSLOT)]
        w_used = sem("w_used")
        xsq = sem("xsq"); xvar = sem("xvar"); xrs = sem("xrs"); xnorm = sem("xnorm")
        xtr = sem("xtr"); xev = sem("xev")
        proj = sem("proj")
        qsq = sem("qsq"); qred = sem("qred"); qvar = sem("qvar"); qrs = sem("qrs"); qnorm = sem("qnorm"); qtr = sem("qtr"); qev = sem("qev")
        gain_ok = sem("gain_ok")
        vev = sem("vev"); v_moved = sem("v_moved")
        win_in = sem("win_in"); bias_ok = sem("bias_ok")
        sc = sem("sc"); smin = sem("smin"); sexp = sem("sexp"); sinv = sem("sinv"); snorm = sem("snorm")
        ptr = sem("ptr"); pev = sem("pev"); pvd = sem("pvd"); oev = sem("oev")
        uev = sem("uev"); cmul = sem("cmul"); cconv = sem("cconv"); bmul = sem("bmul")
        mtile = sem("mtile"); msig = sem("msig"); mmul = sem("mmul"); mixd = sem("mixd")
        e_mm = sem("e_mm"); xe_in = [sem(f"xe_in{i}") for i in range(2)]; e_x1 = sem("e_x1"); e_sq = sem("e_sq"); e_var = sem("e_var"); e_rs = sem("e_rs")
        e_xn = sem("e_xn"); e_tr = sem("e_tr"); e_ht = sem("e_ht"); e_lg = sem("e_lg"); e_lc = sem("e_lc"); e_mx = sem("e_mx"); e_ix = sem("e_ix")
        x1_out = [sem(f"x1_out{i}") for i in range(2)]; h2_out = [sem(f"h2_out{i}") for i in range(2)]
        f_dve = sem("f_dve"); f_dv = sem("f_dv"); f_exp = sem("f_exp"); f_pe = sem("f_pe"); f_bf = sem("f_bf"); table_ok = sem("table_ok")

        g_w = [sem(f"g_w{i}") for i in range(NSLOT)]
        g_mm = [sem(f"g_mm{b}") for b in range(2)]
        g_add = [sem(f"g_add{b}") for b in range(2)]
        g_clip = [sem(f"g_clip{b}") for b in range(2)]
        g_sig = [sem(f"g_sig{b}") for b in range(2)]
        g_m1 = [sem(f"g_m1{b}") for b in range(2)]
        g_act = [sem(f"g_act{b}") for b in range(2)]
        g_atr = [sem(f"g_atr{b}") for b in range(2)]
        g_aev = [sem(f"g_aev{b}") for b in range(2)]
        g_ys = [sem(f"g_ys{b}") for b in range(2)]
        g_sc = [sem(f"g_sc{b}") for b in range(2)]
        g_pick = sem("g_pick"); g_imm = sem("g_imm"); g_ich = sem("g_ich"); g_idx = sem("g_idx"); g_cur = sem("g_cur")
        held = sem("held")
        g_added = sem("g_added"); g_shift = sem("g_shift"); g_col = sem("g_col")
        g_gat = [sem(f"g_gat{b}") for b in range(2)]
        g_xtr = [sem(f"g_xtr{b}") for b in range(2)]
        g_xev = [sem(f"g_xev{b}") for b in range(2)]
        g_brow = sem("g_brow"); g_bgu = sem("g_bgu"); g_bd = sem("g_bd")

        items = []
        wk = A["w_in"].rearrange("(k p) n -> p k n", p=P)
        for c0 in (2048, 1536, 2560):
            for kh in range(2):
                items.append([(wk[:, 4 * kh:4 * kh + 4, c0:c0 + 512], 0, 4, 512)])
        for j in range(4):
            items.append([(wk[:, :, P * j:P * j + P], 0, 8, P), (wk[:, :, 1024 + P * j:1024 + P * j + P], 1024, 8, P)])
            items.append([(wk[:, :, 512 + P * j:512 + P * j + P], 0, 8, P)])
        woc = A["w_oc"].rearrange("(k p) n -> p k n", p=P)
        woa = A["w_oa"].rearrange("(k p) n -> p k n", p=P)
        for d in range(8):
            items.append([(wk[:, :, 3072 + P * d:3072 + P * d + P], 0, 8, P), (wk[:, :, 4096 + P * d:4096 + P * d + P], 1024, 8, P)])
            items.append([(woc[:, :, P * d:P * d + P], 0, 4, P), (woa[:, :, P * d:P * d + P], 512, 4, P)])
        wo = A["w_o"].rearrange("(k p) n -> p k n", p=P)
        for k2 in range(4):
            items.append([(wo[:, 2 * k2:2 * k2 + 2, :], 0, 2, D)])
        NI = len(items)
        landed, total = [], [0] * MSLOT
        for n, it in enumerate(items):
            total[n % MSLOT] += 16 * len(it)
            landed.append(total[n % MSLOT])
        IT_CONV, IT_MERGE, IT_WO = 6, 14, 30

        def item_view(n, off, k, w):
            return ring[:, n % MSLOT, off:off + k * w].rearrange("p (k n) -> p k n", k=k)

        def wait_item(e, n):
            e.wait_ge(w_in[n % MSLOT], landed[n])

        NCONST = 8
        units = HEADS * 8
        unit_end = [(m + 1) * units // 24 for m in range(24)]

        def unit(n):
            h, b = n // 8, n % 8
            rb, cb = b // 4, b % 4
            return h, rb, cb, 3 * rb + COL_VAR[cb]

        def q_evacs(n):
            return n + max(0, n - TT)
        LAST_USE = [0, 2, 3, 4, 6, 7]

        def hold(e, s, value):
            e.wait_ge(s, value)
            e.sem_inc(held, 1)

        block = ctx.enter_context(nc.Block())

        @block.sync
        def _(e):
            for dst, src in ((nmix[:, :], A["nmix"]), (nffn[:, :], A["nffn"]), (convw[:, :], A["convw"]),
                             (gain[:, :], A["qkgain"]), (br_row[:, :], A["b_r"]),
                             (wr[:, :, :], A["w_r"].rearrange("(k p) n -> p k n", p=P)),
                             (masks[:, :, :], A["masks"].rearrange("p (v n) -> p v n", v=6))):
                e.dma_start(dst, src).then_inc(consts_in, 16)
            e.dma_start(xt[0], A["x"][0:P, :]).then_inc(x_in[0], 16)
            e.dma_start(xt[1], A["x"][P:2 * P, :]).then_inc(x_in[1], 16)

            def load_item(n):
                if n >= MSLOT:
                    e.wait_ge(w_used, n - MSLOT + 1)
                for src, off, k, w in items[n]:
                    e.dma_start(item_view(n, off, k, w), src).then_inc(w_in[n % MSLOT], 16)
            load_item(0)
            load_item(1)
            for t in range(2, TT):
                e.wait_ge(xtr, t - 1)
                e.dma_start(xt[t % 2], A["x"][P * t:P * t + P, :]).then_inc(x_in[t % 2], 16)
            for n in range(2, 6):
                load_item(n)
            e.wait_ge(made, 2)
            for dst in (out, h2_rows):
                for r in (S, S + P):
                    e.dma_start(dst[r:r + P, :], oT[:, 0, :]).then_inc(zero_out, 16)
            for n in range(6, 10):
                load_item(n)
            e.wait_ge(vev, TT)
            for cb in range(4):
                for i in range(4):
                    p0 = 64 * (i % 2) + COL_BASE[cb]
                    e.dma_start(vb[32 * i:32 * i + 32, cb, :, :], vnat[p0:p0 + 32, i // 2:TT:2, :]).then_inc(v_moved, 16)
            for n in range(10, NI):
                load_item(n)
            for t in range(TT):
                if t == 0:
                    e.wait_ge(oev, units)
                    e.dma_start(xe[0], A["x"][0:P, :]).then_inc(xe_in[0], 16)
                    e.dma_start(xe[1], A["x"][P:2 * P, :]).then_inc(xe_in[1], 16)
                e.wait_ge(e_x1, 2 * t + 2)
                e.dma_start(out[P * t:P * t + P, :], xe[t % 2]).then_inc(x1_out[t % 2], 16)
                e.wait_ge(e_xn, t + 1)
                e.dma_start(h2_rows[P * t:P * t + P, :], xn[t % 2]).then_inc(h2_out[t % 2], 16)
                if t + 2 < TT:
                    e.wait_ge(x1_out[t % 2], 16 * (t // 2 + 1))
                    e.dma_start(xe[t % 2], A["x"][P * (t + 2):P * (t + 3), :]).then_inc(xe_in[t % 2], 16)

            wg = A["w_gate"].rearrange("e (k p) n -> p e k n", p=P)
            wu = A["w_up"].rearrange("e (k p) n -> p e k n", p=P)
            wd = A["w_down"].rearrange("e (k p) n -> p e k n", p=P)

            def load_half_step(c, ex):
                s, kh = c // 2, c % 2
                view = ring[:, c % NSLOT, :].rearrange("p (k n) -> p k n", k=4)
                if s < 4:
                    for j, w in enumerate((wg, wu)):
                        src = w[:, bass.ds(ex, 1), 4 * kh:4 * kh + 4, FQ * s:FQ * s + FQ].rearrange("p e k n -> p (e k) n")
                        e.dma_start(view[:, :, FQ * j:FQ * j + FQ], src).then_inc(g_w[c % NSLOT], 16)
                else:
                    for j in range(2):
                        src = wd[:, bass.ds(ex, 1), 4 * kh + 2 * j:4 * kh + 2 * j + 2, 512 * (s - 4):512 * (s - 4) + 512].rearrange("p e k n -> p (e k) n")
                        e.dma_start(view[:, 2 * j:2 * j + 2, :], src).then_inc(g_w[c % NSLOT], 16)
            e.wait_ge(w_used, NI)
            e.wait_ge(table_ok, 1)
            n_pass = e.value_load(table[0:1, 3 * NT:3 * NT + 1], min_val=1, max_val=MAX_PASSES)
            ex0 = e.value_load(table[0:1, 0:1], min_val=0, max_val=E - 1)
            for c in range(NSLOT):
                load_half_step(c, ex0)
            with e.Fori(0, n_pass) as p:
                ex = e.value_load(table[0:1, bass.ds(p, 1)], min_val=0, max_val=E - 1)
                hb = e.value_load(table[0:1, bass.ds(p + NT, 1)], min_val=0, max_val=1)
                nb = e.value_load(table[0:1, bass.ds(p + 2 * NT, 1)], min_val=0, max_val=MAX_PASSES)
                for c in range(NSLOT, 12):
                    s = c // 2 - 3
                    hold(e, g_mm[0], 1 + STEPS * p + s + 1)
                    hold(e, g_mm[1], 1 + STEPS * nb + hb * (s + 1))
                    load_half_step(c, ex)
                with e.If(p + 1 < n_pass):
                    exn = e.value_load(table[0:1, bass.ds(p + 1, 1)], min_val=0, max_val=E - 1)
                    for c in range(NSLOT):
                        s = c // 2 + 3
                        hold(e, g_mm[0], 1 + STEPS * p + s + 1)
                        hold(e, g_mm[1], 1 + STEPS * nb + hb * (s + 1))
                        load_half_step(c, exn)
            e.wait_ge(zero_out, 64)
            e.wait_ge(x1_out[0], 16 * TT // 2)
            e.wait_ge(x1_out[1], 16 * TT // 2)

        @block.gpsimd
        def _(e):
            for s in (g_pick, g_shift, g_col, g_bgu, g_bd, g_added):
                e.sem_inc(s, 1)
            e.memset(ident[:, :], 0.0).then_inc(pool_c, 1)
            e.memset(tri_bf[:, :], 1.0).then_inc(pool_c, 1)
            e.memset(ones_bf[:, :], 1.0).then_inc(pool_c, 1)
            e.memset(ones_row[:, :], 1.0).then_inc(pool_c, 1)
            e.memset(half[:, :], -0.5).then_inc(pool_c, 1)
            e.iota(iota_i[:, :], pattern=[[1, SLOTS]], base=0, channel_multiplier=0).then_inc(pool_c, 1)
            e.iota(ctile_i[:, :], pattern=[[P, TT], [0, E]], base=0, channel_multiplier=0).then_inc(pool_c, 1)
            e.iota(cpart_i[:, :], pattern=[[0, TT * E]], base=0, channel_multiplier=1).then_inc(pool_c, 1)
            e.iota(dum_i[:, :], pattern=[[P, 2]], base=DUMMY, channel_multiplier=1).then_inc(pool_c, 1)
            e.wait_ge(pool_c, 9)
            e.affine_select(out=ident[:, :], in_=ident[:, :], compare_op=ALU.not_equal, fill=1.0,
                            base=0, pattern=[[-1, P]], channel_multiplier=1).then_inc(made, 1)
            e.memset(oT[:, 0, :], 0.0).then_inc(made, 1)
            e.affine_select(out=tri_bf[:, :], in_=tri_bf[:, :], compare_op=ALU.is_ge, fill=0.0,
                            base=0, pattern=[[1, P]], channel_multiplier=-1).then_inc(made, 1)
            e.tensor_copy(iota_f[:, :], iota_i[:, :]).then_inc(made, 1)
            e.tensor_copy(dum[:, :], dum_i[:, :]).then_inc(made, 1)
            r2 = rows_bf[:, :, :, :].rearrange("p t e c -> p (t e) c")
            e.tensor_copy(r2[:, :, 0], ctile_i[:, :]).then_inc(made, 1)
            e.tensor_copy(r2[:, :, 1], cpart_i[:, :]).then_inc(made, 1)
            e.memset(r2[:, :, 2], 1.0).then_inc(made, 1)

            for t in range(TT):
                e.wait_ge(xvar, t + 1)
                e.tensor_tensor(rstd[:, t:t + 1], var[:, t:t + 1], half[:, 0:1], ALU.pow).then_inc(xrs, 1)
            for n in range(2 * TT):
                e.wait_ge(qvar, n + 1)
                if n >= 2:
                    e.wait_ge(qnorm, n - 1)
                e.tensor_tensor(rs8[:, n % 2, :], var8[:, n % 2, :], half[:, :], ALU.pow).then_inc(qrs, 1)
            e.wait_ge(consts_in, 16 * (NCONST - 1))
            for h in range(HEADS):
                if h:
                    e.wait_ge(bias_ok, 6 * h)
                e.dma_start(win[:, :, :].rearrange("p r c -> p (r c)")[:, 0:WIN], A["windows"][h, :, :]).then_inc(win_in, 16)
                e.wait_ge(win_in, 16 * (h + 1))
                for v in range(6):
                    rb, cv = v // 3, v % 3
                    r0, c0 = (4, 0)[rb], (16, 8, 0)[cv]
                    if h:
                        e.wait_ge(smin, 8 * (h - 1) + LAST_USE[v] + 1)
                    e.tensor_tensor(bias[:, v, :].rearrange("p (r c) -> p r c", r=KR),
                                    masks[:, v, :].rearrange("p (r c) -> p r c", r=KR),
                                    win[:, r0:r0 + KR, c0:c0 + KC], ALU.subtract).then_inc(bias_ok, 1)
            for t in range(TT):
                e.wait_ge(e_var, t + 1)
                e.tensor_tensor(rstd[:, t:t + 1], var[:, t:t + 1], half[:, 0:1], ALU.pow).then_inc(e_rs, 1)

            e.wait_ge(table_ok, 1)
            e.wait_ge(h2_out[0], 16 * TT // 2)
            e.wait_ge(h2_out[1], 16 * TT // 2)
            e.wait_ge(zero_out, 64)
            e.wait_ge(x1_out[0], 16 * TT // 2)
            e.wait_ge(x1_out[1], 16 * TT // 2)
            n_pass = e.value_load(table[0:1, 3 * NT:3 * NT + 1], min_val=1, max_val=MAX_PASSES)

            def expert_of(n):
                return (e.value_load(table[0:1, bass.ds(n, 1)], min_val=0, max_val=E - 1),
                        e.value_load(table[0:1, bass.ds(n + NT, 1)], min_val=0, max_val=1),
                        e.value_load(table[0:1, bass.ds(n + 2 * NT, 1)], min_val=0, max_val=MAX_PASSES))

            def load_bias_rows(ex):
                for j, b in enumerate((A["b_gate"], A["b_up"])):
                    e.dma_start(brow[0:1, 0:2 * D].rearrange("o (s j n) -> o s j n", s=4, j=2)[:, :, j, :],
                                b[bass.ds(ex, 1), :].rearrange("o (s n) -> o s n", s=4)).then_inc(g_brow, 16)
                e.dma_start(brow[0:1, 2 * D:3 * D], A["b_down"][bass.ds(ex, 1), :]).then_inc(g_brow, 16)

            def pick_tokens(ex, n, shift):
                if shift:
                    hold(e, g_imm, 1 + n)
                    e.tensor_scalar(slot_of[:, :, :], slot_of[:, :, :], float(-SLOTS), None, ALU.add).then_inc(g_shift, 1)
                    hold(e, g_shift, 1 + n)
                e.tensor_copy(slot_col[:, :, :], slot_of[:, :, bass.ds(ex, 1)]).then_inc(g_col, 1)
                hold(e, g_col, 1 + n + 1)
                for t in range(TT):
                    ins = e.tensor_scalar(pick[:, t, :], iota_f[:, :], slot_col[:, t, :], None, ALU.is_equal)
                    ins.then_inc(g_pick, 1)

            def gather(n, hb):
                hold(e, g_idx, 1 + 2 * n + 2)
                hold(e, g_xtr[0], 1 + n)
                e.indirect_dma_start(out=xg[0][:, :], out_offset=None, in_=h2_rows,
                                     in_offset=bass.IndirectOffsetOnAxis(ap=idx_next[:, 0:1], axis=0)).then_inc(g_gat[0], 16)
                with e.If(hb > 0):
                    e.indirect_dma_start(out=xg[1][:, :], out_offset=None, in_=h2_rows,
                                         in_offset=bass.IndirectOffsetOnAxis(ap=idx_next[:, 1:2], axis=0)).then_inc(g_gat[1], 16)

            ex, hb, nb = expert_of(0)
            load_bias_rows(ex)
            pick_tokens(ex, 0, False)
            e.wait_ge(g_brow, 48)
            e.partition_broadcast(bbc[:, 0:2 * D], brow[0:1, 0:2 * D]).then_inc(g_bgu, 1)
            e.partition_broadcast(bbc[:, 2 * D:3 * D], brow[0:1, 2 * D:3 * D]).then_inc(g_bd, 1)
            gather(0, hb)

            with e.Fori(0, n_pass) as p:
                _, hb, nb = expert_of(p)
                exn, hbn, nbn = expert_of(p + 1)

                hold(e, g_bgu, 1 + p + 1)
                hold(e, g_bd, 1 + p + 1)
                load_bias_rows(exn)
                pick_tokens(exn, p + 1, True)
                hold(e, g_xtr[1], 1 + nb + hb)
                gather(p + 1, hbn)
                hold(e, g_brow, 48 * p + 96)
                hold(e, g_add[0], 1 + STEPS * p + 4)
                hold(e, g_add[1], 1 + STEPS * nb + 4 * hb)
                e.partition_broadcast(bbc[:, 0:2 * D], brow[0:1, 0:2 * D]).then_inc(g_bgu, 1)
                hold(e, g_ys[0], 1 + 2 * p + 2)
                hold(e, g_cur, 1 + p + 1)
                e.indirect_dma_start(out=out, out_offset=bass.IndirectOffsetOnAxis(ap=idx_cur[:, 0:1], axis=0),
                                     in_=ys[0][:, :], in_offset=None, compute_op=ALU.add).then_inc(g_sc[0], 16)
                with e.If(hb > 0):
                    hold(e, g_ys[1], 1 + 2 * nb + 2)
                    e.indirect_dma_start(out=out, out_offset=bass.IndirectOffsetOnAxis(ap=idx_cur[:, 1:2], axis=0),
                                         in_=ys[1][:, :], in_offset=None, compute_op=ALU.add).then_inc(g_sc[1], 16)
                hold(e, g_add[0], 1 + STEPS * p + STEPS)
                hold(e, g_add[1], 1 + STEPS * (nb + hb))
                e.partition_broadcast(bbc[:, 2 * D:3 * D], brow[0:1, 2 * D:3 * D]).then_inc(g_bd, 1)
                hold(e, g_sc[0], 16 * p + 16)
                with e.If(hb > 0):
                    hold(e, g_sc[1], 16 * nb + 16)
                e.sem_inc(g_added, 1)

        @block.scalar
        def _(e):
            for s in (*g_sig, *g_aev, *g_ys):
                e.sem_inc(s, 1)
            for t in range(TT):
                e.wait_ge(x_in[t % 2], 16 * (t // 2 + 1))
                if t:
                    e.wait_ge(xsq, t)
                e.activation(junk, xt[t % 2], ACT.Square, accum_out=ss[:, t:t + 1]).then_inc(xsq, 1)
            e.wait_ge(gain_ok, 1)

            def squares(n):
                e.wait_ge(proj, n + 1)
                if n:
                    e.wait_ge(qred, n)
                e.activation(sq, bank[n % 2][:, :], ACT.Square).then_inc(qsq, 1)

            def transposed(n):
                e.wait_ge(qtr, n + 1)
                g, t = n // TT, n % TT
                src = bank[2 + n % 2][:, :].rearrange("p (h t) -> p h t", h=4)
                if g == 0:
                    e.activation(qkT[:, 0:4, P * t:P * t + P], src, ACT.Copy, scale=gain[:, 0:1]).then_inc(qev, 1)
                else:
                    for i in range(2):
                        rb, r = (2 * t + i) // QR, (2 * t + i) % QR
                        dst = qkT[:, 4:8, 512 * rb:512 * rb + 512].rearrange("p h (b q) -> p h b q", b=4)[:, :, :, QC * r:QC * r + QC]
                        ins = e.activation(dst, src[:, :, GRID_W * i:GRID_W * i + GRID_W].rearrange("p h (b c) -> p h b c", b=4),
                                           ACT.Copy, scale=gain[:, 1:2])
                        ins.then_inc(qev, 1)

            for n in range(2 * TT):
                squares(n)
                if n:
                    transposed(n - 1)
            for t in range(TT):
                n = 2 * TT + t
                e.wait_ge(proj, n + 1)
                if t == 0:
                    e.wait_ge(zero_out, 64)
                e.activation(vnat[:, t, :], bank[n % 2][:, :], ACT.Copy).then_inc(vev, 1)
                if t == 0:
                    transposed(n - 1)

            def exps(n):
                e.wait_ge(smin, n + 1)
                e.activation(prob[n % 2], prob[n % 2], ACT.Exp, bias=nmin[:, n % 2:n % 2 + 1], scale=-1.0,
                             accum_out=rsum[:, n % 2:n % 2 + 1]).then_inc(sexp, 1)

            def probs_out(n):
                e.wait_ge(ptr, n + 1)
                if n >= 2:
                    e.wait_ge(pvd, n - 1)
                e.activation(probT[n % 2], bank[4 + n % 2][:, 0:KEYS], ACT.Copy).then_inc(pev, 1)
            un = 0
            for m in range(24):
                j, part, hf = m // 6, (m % 6) // 2, m % 2
                if part == 0:
                    e.wait_ge(proj, 3 * TT + m + 1)
                    if j >= 2:
                        e.wait_ge(cconv, j - 1)
                    e.activation(u[j % 2][:, 512 * hf:512 * hf + 512], bank[m % 2][:, :], ACT.Copy).then_inc(uev, 1)
                while un < unit_end[m]:
                    exps(un)
                    if un:
                        probs_out(un - 1)
                    un += 1
            probs_out(units - 1)

            for n in range(16):
                for g in range(2):
                    e.wait_ge(mtile, 4 * n + g + 1)
                    if n == 0 and g == 0:
                        e.wait_ge(bmul, 8)
                    if n:
                        e.wait_ge(mmul, 2 * (n - 1) + g + 1)
                    e.activation(tmp[g], bank[4 * (n % 2) + g][:, :], ACT.Sigmoid).then_inc(msig, 1)
            for t in range(TT):
                e.wait_ge(e_x1, 2 * t + 2)
                if t:
                    e.wait_ge(e_sq, t)
                e.activation(junk_e, xe[t % 2], ACT.Square, accum_out=ss[:, t:t + 1]).then_inc(e_sq, 1)
            e.wait_ge(f_dv, 1)
            e.activation(ev[:, :, :], ev[:, :, :], ACT.Exp).then_inc(f_exp, 1)

            e.wait_ge(table_ok, 1)
            n_pass = e.value_load(table[0:1, 3 * NT:3 * NT + 1], min_val=1, max_val=MAX_PASSES)
            with e.Fori(0, n_pass) as p:
                hb = e.value_load(table[0:1, bass.ds(p + NT, 1)], min_val=0, max_val=1)
                nb = e.value_load(table[0:1, bass.ds(p + 2 * NT, 1)], min_val=0, max_val=MAX_PASSES)

                def sigmoid(b, s, at):
                    e.wait_ge(g_clip[b], 1 + 8 * at + 2 * s + 1)
                    e.activation(sg[b][:, :], gu[b][:, 0:FQ], ACT.Sigmoid, scale=ALPHA).then_inc(g_sig[b], 1)

                def act_out(b, s, at):
                    e.wait_ge(g_atr[b], 1 + 4 * at + s + 1)
                    e.activation(aT[b][:, 2 * s:2 * s + 2, :], bank[6 + b][:, 0:FQ].rearrange("p (k t) -> p k t", k=2),
                                 ACT.Copy).then_inc(g_aev[b], 1)

                def y_out(b, h, at):
                    e.wait_ge(g_add[b], 1 + STEPS * at + 4 + h + 1)
                    if h == 0:
                        e.wait_ge(g_added, 1 + p)
                        e.wait_ge(g_cur, 1 + p + 1)
                    e.activation(ys[b][:, 512 * h:512 * h + 512], yt[b][:, :], ACT.Copy, scale=gate_cur[:, b:b + 1]).then_inc(g_ys[b], 1)

                for s in range(4):
                    sigmoid(0, s, p)
                    with e.If(hb > 0):
                        sigmoid(1, s, nb)
                    if s:
                        act_out(0, s - 1, p)
                        with e.If(hb > 0):
                            act_out(1, s - 1, nb)
                act_out(0, 3, p)
                with e.If(hb > 0):
                    act_out(1, 3, nb)
                for h in range(2):
                    y_out(0, h, p)
                    with e.If(hb > 0):
                        y_out(1, h, nb)

        @block.vector
        def _(e):
            for s in (*g_add, *g_clip, *g_m1, *g_act, *g_xev, g_ich, g_idx, g_cur):
                e.sem_inc(s, 1)
            e.wait_ge(consts_in, 16 * (NCONST - 1))
            e.tensor_scalar(gain[:, 1:2], gain[:, 1:2], -float(HD) ** -0.5, None, ALU.mult).then_inc(gain_ok, 1)

            def x_evac(t):
                e.wait_ge(xtr, t + 1)
                for i in range(2):
                    e.tensor_tensor(hT[:, 4 * i:4 * i + 4, P * t:P * t + P],
                                    bank[4 + 2 * (t % 2) + i][:, :].rearrange("p (k t) -> p k t", k=4),
                                    nmix[:, 4 * i:4 * i + 4, None].to_broadcast([P, 4, P]), ALU.mult).then_inc(xev, 1)
            for t in range(TT):
                e.wait_ge(xsq, t + 1)
                e.tensor_scalar(var[:, t:t + 1], ss[:, t:t + 1], 1.0 / D, EPS, ALU.mult, ALU.add).then_inc(xvar, 1)
                e.wait_ge(xrs, t + 1)
                e.tensor_scalar(xt[t % 2], xt[t % 2], rstd[:, t:t + 1], None, ALU.mult).then_inc(xnorm, 1)
                if t:
                    x_evac(t - 1)
            x_evac(TT - 1)
            for n in range(2 * TT):
                e.wait_ge(qsq, n + 1)
                e.tensor_reduce(ss8[:, n % 2, :], sq.rearrange("p (h d) -> p h d", h=HEADS), AX.X, ALU.add).then_inc(qred, 1)
                e.wait_ge(qred, n + 1)
                if n >= 2:
                    e.wait_ge(qrs, n - 1)
                e.tensor_scalar(var8[:, n % 2, :], ss8[:, n % 2, :], 1.0 / HD, EPS, ALU.mult, ALU.add).then_inc(qvar, 1)
                e.wait_ge(qrs, n + 1)
                if n >= 2:
                    e.wait_ge(qtr, n - 1)
                e.tensor_tensor(qn[n % 2].rearrange("p (h d) -> p h d", h=HEADS),
                                bank[n % 2][:, :].rearrange("p (h d) -> p h d", h=HEADS),
                                rs8[:, n % 2, :, None].to_broadcast([P, HEADS, HD]), ALU.mult).then_inc(qnorm, 1)

            def min_of(n):
                h, rb, cb, v = unit(n)
                e.wait_ge(sc, n + 1)
                e.wait_ge(bias_ok, 6 * h + v + 1)
                if n >= 2:
                    e.wait_ge(ptr, n - 1)
                if n == 0:
                    e.wait_ge(qtr, 2 * TT)
                e.tensor_tensor_reduce(out=prob[n % 2], in0=bank[2 + n % 2][:, 0:KEYS], in1=bias[:, v, :], scale=1.0,
                                       scalar=3.0e38, op0=ALU.add, op1=ALU.min, accum_out=nmin[:, n % 2:n % 2 + 1]).then_inc(smin, 1)

            def normalise(n):
                e.wait_ge(sexp, n + 1)
                e.reciprocal(rinv[:, n % 2:n % 2 + 1], rsum[:, n % 2:n % 2 + 1]).then_inc(sinv, 1)
                e.wait_ge(sinv, n + 1)
                e.tensor_scalar(prob[n % 2], prob[n % 2], rinv[:, n % 2:n % 2 + 1], None, ALU.mult).then_inc(snorm, 1)

            def attn_out(n):
                h, rb, cb, v = unit(n)
                e.wait_ge(pvd, n + 1)
                if n == 0:
                    e.wait_ge(v_moved, 256)
                h0 = HD * (h % 2)
                dst = oT[h0:h0 + HD, h // 2, :].rearrange("p (r c) -> p r c", c=GRID_W)
                e.tensor_copy(dst[:, QR * rb:QR * rb + QR, QC * cb:QC * cb + QC],
                              bank[6 + n % 2][h0:h0 + HD, 0:P].rearrange("p (r c) -> p r c", c=QC)).then_inc(oev, 1)
            un = 0
            for m in range(24):
                j, part, hf = m // 6, (m % 6) // 2, m % 2
                cols = slice(512 * hf, 512 * hf + 512)
                if part == 1:
                    e.wait_ge(proj, 3 * TT + m + 1)
                    e.wait_ge(uev, 2 * j + hf + 1)
                    e.tensor_tensor(u[j % 2][:, cols], bank[m % 2][:, :], u[j % 2][:, cols], ALU.mult).then_inc(cmul, 1)
                if part == 1 and hf == 1:
                    y, uu = ypre[:, j, :], u[j % 2]
                    e.wait_ge(cmul, 2 * j + 2)
                    e.tensor_scalar(y, uu, convw[:, 4 + j:5 + j], None, ALU.mult).then_inc(f_dve, 1)
                    e.wait_ge(f_dve, 2 * j + 1)
                    e.scalar_tensor_tensor(out=y[:, 1:S], in0=uu[:, 0:S - 1], scalar=convw[:, j:j + 1], in1=y[:, 1:S],
                                           op0=ALU.mult, op1=ALU.add).then_inc(f_dve, 1)
                    e.wait_ge(f_dve, 2 * j + 2)
                    e.scalar_tensor_tensor(out=y[:, 0:S - 1], in0=uu[:, 1:S], scalar=convw[:, 8 + j:9 + j], in1=y[:, 0:S - 1],
                                           op0=ALU.mult, op1=ALU.add).then_inc(cconv, 1)
                if part == 2:
                    e.wait_ge(proj, 3 * TT + m + 1)
                    e.wait_ge(cconv, j + 1)
                    e.tensor_tensor(ypre[:, j, cols], bank[m % 2][:, :], ypre[:, j, cols], ALU.mult).then_inc(bmul, 1)
                while un < unit_end[m]:
                    min_of(un)
                    if un >= 2:
                        attn_out(un - 2)
                    normalise(un)
                    un += 1
            attn_out(units - 2)
            attn_out(units - 1)

            for n in range(16):
                d, hf = n // 2, n % 2
                for g in range(2):
                    e.wait_ge(msig, 2 * n + g + 1)
                    e.wait_ge(mtile, 4 * n + 2 + g + 1)
                    if n:
                        e.wait_ge(mixd, n)
                    e.tensor_tensor(tmp[2 + g], bank[4 * (n % 2) + 2 + g][:, :], tmp[g], ALU.mult).then_inc(mmul, 1)
                e.wait_ge(mmul, 2 * n + 2)
                e.tensor_tensor(mixedT[:, d, 512 * hf:512 * hf + 512], tmp[2], tmp[3], ALU.add).then_inc(mixd, 1)

            def h2_evac(t):
                e.wait_ge(e_tr, t + 1)
                if t >= 2:
                    e.wait_ge(e_lg, t - 1)
                for i in range(2):
                    e.tensor_tensor(h2T[t % 2][:, 4 * i:4 * i + 4, :],
                                    bank[4 + i][:, :].rearrange("p (k t) -> p k t", k=4),
                                    nffn[:, 4 * i:4 * i + 4, None].to_broadcast([P, 4, P]), ALU.mult).then_inc(e_ht, 1)

            def top(t):
                e.wait_ge(e_lg, t + 1)
                e.tensor_copy(logits[:, t, :], bank[6 + t % 2][:, 0:E]).then_inc(e_lc, 1)
                e.wait_ge(e_lc, t + 1)
                e.max(out=top_v[:, t, :], in_=logits[:, t, :]).then_inc(e_mx, 1)
                e.wait_ge(e_mx, t + 1)
                e.max_index(out=top_i[:, t, :], in_max=top_v[:, t, :], in_values=logits[:, t, :]).then_inc(e_ix, 1)
            for t in range(TT):
                e.wait_ge(xe_in[t % 2], 16 * (t // 2 + 1))
                for i in range(2):
                    e.wait_ge(e_mm, 2 * t + i + 1)
                    e.tensor_tensor(xe[t % 2][:, 512 * i:512 * i + 512], bank[2 * (t % 2) + i][:, :],
                                    xe[t % 2][:, 512 * i:512 * i + 512], ALU.add).then_inc(e_x1, 1)
                e.wait_ge(e_sq, t + 1)
                e.tensor_scalar(var[:, t:t + 1], ss[:, t:t + 1], 1.0 / D, EPS, ALU.mult, ALU.add).then_inc(e_var, 1)
                e.wait_ge(e_rs, t + 1)
                if t >= 2:
                    e.wait_ge(h2_out[t % 2], 16 * (t // 2))
                    e.wait_ge(e_tr, t - 1)
                if t == 0:
                    e.wait_ge(mixd, 16)
                e.tensor_scalar(xn[t % 2], xe[t % 2], rstd[:, t:t + 1], None, ALU.mult).then_inc(e_xn, 1)
                if t:
                    h2_evac(t - 1)
                if t >= 2:
                    top(t - 2)
            h2_evac(TT - 1)
            top(TT - 2)
            top(TT - 1)

            chain = [8]

            def link(ins):
                chain[0] += 1
                ins.then_inc(f_dve, 1)
                e.wait_ge(f_dve, chain[0])
            e.wait_ge(e_ix, TT)
            e.wait_ge(made, 8)
            e.wait_ge(h2_out[0], 16 * TT // 2)
            e.wait_ge(h2_out[1], 16 * TT // 2)
            e.wait_ge(x1_out[0], 16 * TT // 2)
            e.wait_ge(x1_out[1], 16 * TT // 2)
            e.tensor_tensor(ev[:, :, :], top_v[:, :, 0:TOPK], top_v[:, :, 0:1].to_broadcast([P, TT, TOPK]), ALU.subtract).then_inc(f_dv, 1)
            link(e.tensor_copy(topi_f[:, :, :], top_i[:, :, 0:TOPK]))
            link(e.tensor_tensor(oh[:, :, :], iota_f[:, None, 0:E].to_broadcast([P, TT * TOPK, E]),
                                 topi_f[:, :, :].rearrange("p t k -> p (t k)")[:, :, None].to_broadcast([P, TT * TOPK, E]), ALU.is_equal))
            oh4 = oh[:, :, :].rearrange("p (t k) e -> p t k e", k=TOPK)
            ohg4 = ohg[:, :, :].rearrange("p (t k) e -> p t k e", k=TOPK)
            r3 = [rt[:, i, :].rearrange("p (t e) -> p t e", t=TT) for i in range(5)]
            e.tensor_tensor(r3[0], oh4[:, :, 0, :], oh4[:, :, 1, :], ALU.add)
            link(e.tensor_tensor(r3[1], oh4[:, :, 2, :], oh4[:, :, 3, :], ALU.add))
            link(e.tensor_tensor(r3[2], r3[0], r3[1], ALU.add))
            e.tensor_copy(routed_bf[:, :], rt[:, 2, :]).then_inc(f_bf, 1)
            e.wait_ge(f_exp, 1)
            link(e.tensor_reduce(esum[:, :], ev[:, :, :], AX.X, ALU.add))
            link(e.reciprocal(esum[:, :], esum[:, :]))
            link(e.tensor_tensor(gk[:, :, :], ev[:, :, :], esum[:, :, None].to_broadcast([P, TT, TOPK]), ALU.mult))
            link(e.tensor_tensor(ohg[:, :, :], oh[:, :, :],
                                 gk[:, :, :].rearrange("p t k -> p (t k)")[:, :, None].to_broadcast([P, TT * TOPK, E]), ALU.mult))
            e.tensor_tensor(r3[0], ohg4[:, :, 0, :], ohg4[:, :, 1, :], ALU.add)
            link(e.tensor_tensor(r3[1], ohg4[:, :, 2, :], ohg4[:, :, 3, :], ALU.add))
            link(e.tensor_tensor(r3[3], r3[0], r3[1], ALU.add))
            link(e.tensor_copy(rows_bf[:, :, :, 3], r3[3]))
            link(e.tensor_tensor(r3[0], r3[3], rows_bf[:, :, :, 3], ALU.subtract))
            link(e.tensor_copy(rows_bf[:, :, :, 4], r3[0]))
            link(e.tensor_tensor(rows_bf[:, :, :, 5], r3[0], rows_bf[:, :, :, 4], ALU.subtract))
            link(e.memset(before[:, 0, :], 0.0))
            e.wait_ge(f_pe, 2)
            for t in range(TT):
                link(e.tensor_tensor(before[:, t + 1, :], bank[1][:, E * t:E * t + E], before[:, t, :], ALU.add))
            count = before[:, TT, :]
            link(e.tensor_scalar(npass[:, :], count, 0.0, None, ALU.is_gt))
            for i in range(1, S // SLOTS):
                link(e.scalar_tensor_tensor(out=npass[:, :], in0=count, scalar=float(SLOTS * i), in1=npass[:, :], op0=ALU.is_gt, op1=ALU.add))
            link(e.memset(scan[:, :, :], 0.0))
            link(e.tensor_copy(scan[:, 0, 16:], npass[:, :]))
            cur = 0
            for d in (1, 2, 4, 8, 16):
                link(e.tensor_tensor(scan[:, 1 - cur, 16:], scan[:, cur, 16:], scan[:, cur, 16 - d:16 + E - d], ALU.add))
                cur = 1 - cur
            pinc = scan[:, cur, 16:]
            link(e.tensor_tensor(pexc[:, :], pinc, npass[:, :], ALU.subtract))
            link(e.tensor_scalar(pexc[:, :], pexc[:, :], float(SLOTS), None, ALU.mult))
            link(e.tensor_tensor(r3[0], bank[0][:, 0:TT * E].rearrange("p (t e) -> p t e", t=TT), before[:, 0:TT, :], ALU.add))
            link(e.tensor_tensor(r3[1], r3[0], pexc[:, None, :].to_broadcast([P, TT, E]), ALU.add))
            link(e.tensor_tensor(r3[4], r3[1], r3[2], ALU.mult))
            link(e.tensor_scalar(slot_of[:, :, :], r3[4], -1.0, None, ALU.add))
            one = slice(0, 1)
            ids = iota_f[one, 0:NT]
            link(e.tensor_tensor(big1[:, :, :], pinc[one, None, :].to_broadcast([1, NT, E]), ids[:, :, None].to_broadcast([1, NT, E]), ALU.is_le))
            link(e.tensor_reduce(row1[:, 0, :], big1[:, :, :], AX.X, ALU.add))
            link(e.tensor_tensor(big1[:, :, :], iota_f[one, None, 0:E].to_broadcast([1, NT, E]), row1[:, 0, :, None].to_broadcast([1, NT, E]), ALU.is_equal))
            link(e.tensor_tensor(row1[:, 5, 0:E], count[one, :], pexc[one, :], ALU.add))
            link(e.tensor_tensor(big2[:, :, :], big1[:, :, :], row1[:, 5, None, 0:E].to_broadcast([1, NT, E]), ALU.mult))
            link(e.tensor_reduce(row1[:, 1, :], big2[:, :, :], AX.X, ALU.add))
            link(e.scalar_tensor_tensor(out=row1[:, 2, :], in0=ids, scalar=float(-SLOTS), in1=row1[:, 1, :], op0=ALU.mult, op1=ALU.add))
            link(e.tensor_scalar(row1[:, 3, :], row1[:, 2, :], float(P), None, ALU.is_gt))
            link(e.memset(scanb[:, :, :], 0.0))
            link(e.tensor_copy(scanb[:, 0, 64:], row1[:, 3, :]))
            cur = 0
            for d in (1, 2, 4, 8, 16, 32):
                link(e.tensor_tensor(scanb[:, 1 - cur, 64:], scanb[:, cur, 64:], scanb[:, cur, 64 - d:64 + NT - d], ALU.add))
                cur = 1 - cur
            link(e.tensor_scalar(table[:, 0:NT], row1[:, 0, :], float(E - 1), None, ALU.min))
            link(e.tensor_copy(table[:, NT:2 * NT], row1[:, 3, :]))
            link(e.tensor_tensor(table[:, 2 * NT:3 * NT], scanb[:, cur, 64:], row1[:, 3, :], ALU.subtract))
            link(e.tensor_copy(table[:, 3 * NT:], pinc[one, E - 1:E]))
            e.sem_inc(table_ok, 1)

            n_pass = e.value_load(table[0:1, 3 * NT:3 * NT + 1], min_val=1, max_val=MAX_PASSES)

            def row_numbers(n):
                e.wait_ge(g_imm, 1 + n + 1)
                k = 4 * n
                e.tensor_copy(islot[:, :], bank[4][:, 0:12]).then_inc(g_ich, 1)
                e.wait_ge(g_ich, 1 + k + 1)
                i6 = islot[:, :].rearrange("p (b c) -> p b c", b=2)
                e.tensor_tensor(itmp[:, 0, :], i6[:, :, 0], i6[:, :, 1], ALU.add)
                e.tensor_tensor(gsum[:, :], i6[:, :, 3], i6[:, :, 4], ALU.add)
                e.tensor_tensor(itmp[:, 1, :], i6[:, :, 2], dum[:, :], ALU.mult).then_inc(g_ich, 1)
                e.wait_ge(g_ich, 1 + k + 2)
                e.tensor_tensor(itmp[:, 2, :], dum[:, :], itmp[:, 1, :], ALU.subtract).then_inc(g_ich, 1)
                e.wait_ge(g_ich, 1 + k + 3)
                e.tensor_tensor(idx_next[:, :], itmp[:, 0, :], itmp[:, 2, :], ALU.add).then_inc(g_idx, 1)
                e.tensor_tensor(gate_next[:, :], gsum[:, :], i6[:, :, 5], ALU.add).then_inc(g_idx, 1)
                e.sem_inc(g_ich, 1)

            def x_evac2(b, at):
                e.wait_ge(g_xtr[b], 1 + at + 1)
                for i in range(2):
                    e.tensor_tensor(xT[b][:, 4 * i:4 * i + 4, :], bank[4 + i][:, :].rearrange("p (k t) -> p k t", k=4),
                                    nffn[:, 4 * i:4 * i + 4, None].to_broadcast([P, 4, P]), ALU.mult).then_inc(g_xev[b], 1)

            row_numbers(0)
            x_evac2(0, 0)
            hb0 = e.value_load(table[0:1, NT:NT + 1], min_val=0, max_val=1)
            with e.If(hb0 > 0):
                x_evac2(1, 0)
            with e.Fori(0, n_pass) as p:
                hb = e.value_load(table[0:1, bass.ds(p + NT, 1)], min_val=0, max_val=1)
                nb = e.value_load(table[0:1, bass.ds(p + 2 * NT, 1)], min_val=0, max_val=MAX_PASSES)
                hbn = e.value_load(table[0:1, bass.ds(p + 1 + NT, 1)], min_val=0, max_val=1)

                def add_bias(b, s, at):
                    e.wait_ge(g_mm[b], 1 + STEPS * at + s + 1)
                    if s < 4:
                        if s == 0:
                            e.wait_ge(g_bgu, 1 + p + 1)
                        e.wait_ge(g_act[b], 1 + 4 * at + s)
                        e.tensor_tensor(gu[b][:, :], bank[2 * b + s % 2][:, :], bbc[:, 2 * FQ * s:2 * FQ * s + 2 * FQ], ALU.add).then_inc(g_add[b], 1)
                    else:
                        e.wait_ge(g_bd, 1 + p + 1)
                        e.wait_ge(g_ys[b], 1 + 2 * at + s - 4)
                        e.tensor_tensor(yt[b][:, :], bank[2 * b + s % 2][:, :], bbc[:, 2 * D + 512 * (s - 4):2 * D + 512 * (s - 4) + 512], ALU.add).then_inc(g_add[b], 1)

                def clip(b, s, at):
                    e.wait_ge(g_add[b], 1 + STEPS * at + s + 1)
                    e.tensor_scalar(gu[b][:, 0:FQ], gu[b][:, 0:FQ], LIMIT, None, ALU.min).then_inc(g_clip[b], 1)
                    e.tensor_scalar(gu[b][:, FQ:2 * FQ], gu[b][:, FQ:2 * FQ], LIMIT, -LIMIT, ALU.min, ALU.max).then_inc(g_clip[b], 1)

                def swiglu(b, s, at):
                    e.wait_ge(g_sig[b], 1 + 4 * at + s + 1)
                    e.tensor_tensor(sg[b][:, :], gu[b][:, 0:FQ], sg[b][:, :], ALU.mult).then_inc(g_m1[b], 1)
                    e.wait_ge(g_m1[b], 1 + 4 * at + s + 1)
                    e.wait_ge(g_clip[b], 1 + 8 * at + 2 * s + 2)
                    e.wait_ge(g_atr[b], 1 + 4 * at + s)
                    e.scalar_tensor_tensor(out=act[b][:, :], in0=gu[b][:, FQ:2 * FQ], scalar=1.0, in1=sg[b][:, :],
                                           op0=ALU.add, op1=ALU.mult).then_inc(g_act[b], 1)

                for s in range(STEPS):
                    add_bias(0, s, p)
                    if s < 4:
                        clip(0, s, p)
                        swiglu(0, s, p)
                    with e.If(hb > 0):
                        add_bias(1, s, nb)
                        if s < 4:
                            clip(1, s, nb)
                            swiglu(1, s, nb)
                    if s == 1:
                        e.wait_ge(g_added, 1 + p)
                        e.tensor_copy(idx_cur[:, :], idx_next[:, :])
                        e.tensor_copy(gate_cur[:, :], gate_next[:, :]).then_inc(g_cur, 1)
                        e.wait_ge(g_cur, 1 + p + 1)
                        row_numbers(p + 1)
                    if s == 4:
                        x_evac2(0, p + 1)
                with e.If(hbn > 0):
                    x_evac2(1, nb + hb)

        @block.tensor
        def _(e):
            for s in (*g_mm, *g_atr, *g_xtr, g_imm):
                e.sem_inc(s, 1)
            e.wait_ge(made, 1)

            def x_transpose(t):
                e.wait_ge(xnorm, t + 1)
                if t >= 2:
                    e.wait_ge(xev, 2 * (t - 1))
                for k in range(KT):
                    i = e.transpose(bank[4 + 2 * (t % 2) + k // 4][:, P * (k % 4):P * (k % 4) + P], xt[t % 2][:, P * k:P * k + P], ident[:, :])
                i.then_inc(xtr, 1)
            for t in range(TT):
                x_transpose(t)

            def q_transpose(n):
                e.wait_ge(qnorm, n + 1)
                if n >= 2:
                    e.wait_ge(qev, q_evacs(n - 1))
                for i in range(4):
                    ins = e.transpose(bank[2 + n % 2][:, P * i:P * i + P], qn[n % 2][:, P * i:P * i + P], ident[:, :])
                ins.then_inc(qtr, 1)
            for g in range(3):
                for t in range(TT):
                    n = TT * g + t
                    if n < TT:
                        e.wait_ge(xev, 2 * t + 2)
                    if n >= 2:
                        if n - 2 < 2 * TT:
                            e.wait_ge(qnorm, n - 1)
                        else:
                            e.wait_ge(vev, n - 2 - 2 * TT + 1)
                    for k in range(KT):
                        if k % 4 == 0:
                            wait_item(e, 2 * g + k // 4)
                        ins = e.matmul(bank[n % 2][:, :], hT[:, k, P * t:P * t + P], item_view(2 * g + k // 4, 0, 4, 512)[:, k % 4, :],
                                       start=(k == 0), stop=(k == KT - 1))
                    ins.then_inc(proj, 1)
                    if 1 <= n <= 2 * TT:
                        q_transpose(n - 1)
                e.wait_ge(proj, TT * (g + 1))
                e.sem_inc(w_used, 2)

            def scores(n):
                h, rb, cb, v = unit(n)
                if n < 2:
                    e.wait_ge(qev, q_evacs(2 * TT))
                else:
                    e.wait_ge(smin, n - 1)
                h0 = HD * (h % 2)
                kg = qkT[h0:h0 + HD, h // 2, :].rearrange("p (r c) -> p r c", c=GRID_W)
                q0 = 512 * rb + P * cb
                e.matmul(bank[2 + n % 2][:, 0:KEYS].rearrange("p (r c) -> p r c", c=KC),
                         qkT[h0:h0 + HD, 4 + h // 2, q0:q0 + P],
                         kg[:, ROW_BASE[rb]:ROW_BASE[rb] + KR, COL_BASE[cb]:COL_BASE[cb] + KC], start=True, stop=True).then_inc(sc, 1)

            def prob_transpose(n):
                e.wait_ge(snorm, n + 1)
                if n >= 2:
                    e.wait_ge(pev, n - 1)
                for i in range(3):
                    ins = e.transpose(bank[4 + n % 2][:, P * i:P * i + P], prob[n % 2][:, P * i:P * i + P], ident[:, :])
                ins.then_inc(ptr, 1)

            def weighted(n):
                h, rb, cb, v = unit(n)
                e.wait_ge(pev, n + 1)
                if n == 0:
                    e.wait_ge(v_moved, 256)
                if n >= 2:
                    e.wait_ge(oev, n - 1)
                h0 = HD * (h % 2)
                for i in range(3):
                    ins = e.matmul(bank[6 + n % 2][h0:h0 + HD, 0:P], vb[:, cb, rb + i, HD * h:HD * h + HD],
                                   probT[n % 2][:, P * i:P * i + P], start=(i == 0), stop=(i == 2))
                ins.then_inc(pvd, 1)
            un = 0
            for m in range(24):
                j, part, hf = m // 6, (m % 6) // 2, m % 2
                it = IT_CONV + 2 * j + (part == 2)
                wait_item(e, it)
                wv = item_view(it, 1024 if part == 1 else 0, 8, P)
                if m < 2:
                    e.wait_ge(vev, TT - 1 + m)
                else:
                    jj, pp, hh = (m - 2) // 6, ((m - 2) % 6) // 2, (m - 2) % 2
                    e.wait_ge((uev, cmul, bmul)[pp], 2 * jj + hh + 1)
                for k in range(KT):
                    ins = e.matmul(bank[m % 2][:, :], wv[:, k, :], hT[:, k, 512 * hf:512 * hf + 512], start=(k == 0), stop=(k == KT - 1))
                ins.then_inc(proj, 1)
                if (part, hf) in ((1, 1), (2, 1)):
                    e.wait_ge(proj, 3 * TT + m + 1)
                    e.sem_inc(w_used, 1)
                while un < unit_end[m]:
                    scores(un)
                    if un >= 1:
                        prob_transpose(un - 1)
                    if un >= 2:
                        weighted(un - 2)
                    un += 1
            prob_transpose(units - 1)
            weighted(units - 2)
            weighted(units - 1)

            for n in range(16):
                d, hf = n // 2, n % 2
                cols = slice(512 * hf, 512 * hf + 512)
                b0 = 4 * (n % 2)
                if n == 0:
                    e.wait_ge(bmul, 8)
                    e.wait_ge(smin, units)
                elif n == 1:
                    e.wait_ge(pev, units)
                    e.wait_ge(oev, units)
                else:
                    e.wait_ge(mmul, 2 * (n - 1))
                wait_item(e, IT_MERGE + 2 * d)
                for g in range(2):
                    for k in range(KT):
                        ins = e.matmul(bank[b0 + g][:, :], item_view(IT_MERGE + 2 * d, 1024 * g, 8, P)[:, k, :], hT[:, k, cols],
                                       start=(k == 0), stop=(k == KT - 1))
                    ins.then_inc(mtile, 1)
                wait_item(e, IT_MERGE + 2 * d + 1)
                if n == 0:
                    e.wait_ge(oev, units)
                for g, src in enumerate((ypre, oT)):
                    for k in range(4):
                        ins = e.matmul(bank[b0 + 2 + g][:, :], item_view(IT_MERGE + 2 * d + 1, 512 * g, 4, P)[:, k, :], src[:, k, cols],
                                       start=(k == 0), stop=(k == 3))
                    ins.then_inc(mtile, 1)
                if hf == 1:
                    e.wait_ge(mtile, 4 * n + 4)
                    e.sem_inc(w_used, 2)

            def h2_transpose(t):
                e.wait_ge(e_xn, t + 1)
                if t:
                    e.wait_ge(e_ht, 2 * t)
                for k in range(KT):
                    ins = e.transpose(bank[4 + k // 4][:, P * (k % 4):P * (k % 4) + P], xn[t % 2][:, P * k:P * k + P], ident[:, :])
                ins.then_inc(e_tr, 1)

            def router(t):
                e.wait_ge(e_ht, 2 * t + 2)
                if t >= 2:
                    e.wait_ge(e_lc, t - 1)
                dst = bank[6 + t % 2][:, 0:E]
                for k in range(KT):
                    e.matmul(dst, h2T[t % 2][:, k, :], wr[:, k, :], start=(k == 0), stop=False)
                e.matmul(dst, ones_row[0:1, :], br_row[0:1, :], start=False, stop=True).then_inc(e_lg, 1)
            for t in range(TT):
                if t == 0:
                    e.wait_ge(mixd, 16)
                if t >= 2:
                    e.wait_ge(e_x1, 2 * (t - 1))
                for i in range(2):
                    for k in range(KT):
                        if t == 0 and i == 0 and k % 2 == 0:
                            wait_item(e, IT_WO + k // 2)
                        ins = e.matmul(bank[2 * (t % 2) + i][:, :], mixedT[:, k, P * t:P * t + P],
                                       item_view(IT_WO + k // 2, 0, 2, D)[:, k % 2, 512 * i:512 * i + 512], start=(k == 0), stop=(k == KT - 1))
                    ins.then_inc(e_mm, 1)
                if t:
                    h2_transpose(t - 1)
                if t >= 2:
                    router(t - 2)
            e.wait_ge(e_mm, 2 * TT)
            e.sem_inc(w_used, 4)
            h2_transpose(TT - 1)
            router(TT - 2)
            router(TT - 1)

            e.wait_ge(f_bf, 1)
            e.wait_ge(e_x1, 2 * TT)
            e.matmul(bank[0][:, 0:TT * E], tri_bf[:, :], routed_bf[:, :], start=True, stop=True).then_inc(f_pe, 1)
            e.matmul(bank[1][:, 0:TT * E], ones_bf[:, :], routed_bf[:, :], start=True, stop=True).then_inc(f_pe, 1)

            e.wait_ge(table_ok, 1)
            n_pass = e.value_load(table[0:1, 3 * NT:3 * NT + 1], min_val=1, max_val=MAX_PASSES)

            def slot_rows(ex, n):
                e.wait_ge(g_pick, 1 + TT * n + TT)
                for b in range(2):
                    for t in range(TT):
                        ins = e.matmul(bank[4][:, 6 * b:6 * b + 6], pick[:, t, P * b:P * b + P],
                                       rows_bf[:, t, bass.ds(ex, 1), :].rearrange("p e c -> p (e c)"), start=(t == 0), stop=(t == TT - 1))
                ins.then_inc(g_imm, 1)

            def rows_transpose(b, at, n):
                e.wait_ge(g_gat[b], 16 * at + 16)
                for k in range(KT):
                    ins = e.transpose(bank[4 + k // 4][:, P * (k % 4):P * (k % 4) + P], xg[b][:, P * k:P * k + P], ident[:, :])
                ins.then_inc(g_xtr[b], 1)

            ex = e.value_load(table[0:1, 0:1], min_val=0, max_val=E - 1)
            hb = e.value_load(table[0:1, NT:NT + 1], min_val=0, max_val=1)
            slot_rows(ex, 0)
            rows_transpose(0, 0, 0)
            with e.If(hb > 0):
                e.wait_ge(g_xev[0], 1 + 2)
                rows_transpose(1, 0, 0)
            with e.Fori(0, n_pass) as p:
                hb = e.value_load(table[0:1, bass.ds(p + NT, 1)], min_val=0, max_val=1)
                nb = e.value_load(table[0:1, bass.ds(p + 2 * NT, 1)], min_val=0, max_val=MAX_PASSES)
                exn = e.value_load(table[0:1, bass.ds(p + 1, 1)], min_val=0, max_val=E - 1)
                hbn = e.value_load(table[0:1, bass.ds(p + 1 + NT, 1)], min_val=0, max_val=1)

                def step(b, s, at, ks=range(KT), last=True):
                    if 0 in ks:
                        e.wait_ge(g_add[b], 1 + STEPS * at + max(s - 1, 0))
                        if s == 0:
                            e.wait_ge(g_xev[b], 1 + 2 * at + 2)
                    if s >= 4:
                        e.wait_ge(g_aev[b], 1 + 4 * at + (4 if 6 in ks else 3))
                    src = xT[b] if s < 4 else aT[b]
                    for k in ks:
                        w = ring[:, (2 * s + k // 4) % NSLOT, :].rearrange("p (k n) -> p k n", k=4)
                        if b == 0 and k % 4 == 0:
                            e.wait_ge(g_w[(2 * s + k // 4) % NSLOT], 64 * p + 32 * ((2 * s + k // 4) // NSLOT) + 32)
                        ins = e.matmul(bank[2 * b + s % 2][:, :], src[:, k, :], w[:, k % 4, :], start=(k == 0), stop=(k == KT - 1))
                    if last:
                        ins.then_inc(g_mm[b], 1)

                def act_transpose(b, s, at):
                    e.wait_ge(g_act[b], 1 + 4 * at + s + 1)
                    e.wait_ge(g_aev[b], 1 + 4 * at + s)
                    for k in range(2):
                        ins = e.transpose(bank[6 + b][:, P * k:P * k + P], act[b][:, P * k:P * k + P], ident[:, :])
                    ins.then_inc(g_atr[b], 1)

                for s in range(4):
                    step(0, s, p)
                    with e.If(hb > 0):
                        step(1, s, nb)
                    if s:
                        act_transpose(0, s - 1, p)
                        with e.If(hb > 0):
                            act_transpose(1, s - 1, nb)
                    if s == 2:
                        slot_rows(exn, p + 1)
                step(0, 4, p, range(6), False)
                act_transpose(0, 3, p)
                with e.If(hb > 0):
                    step(1, 4, nb, range(6), False)
                    act_transpose(1, 3, nb)
                step(0, 4, p, range(6, 8))
                with e.If(hb > 0):
                    step(1, 4, nb, range(6, 8))
                e.wait_ge(g_xev[1], 1 + 2 * (nb + hb))
                rows_transpose(0, p + 1, p + 1)
                step(0, 5, p)
                with e.If(hb > 0):
                    step(1, 5, nb)
                with e.If(hbn > 0):
                    e.wait_ge(g_xev[0], 1 + 2 * p + 4)
                    rows_transpose(1, nb + hb, p + 1)


_INPUTS = ["x", "nmix", "w_in", "convw", "w_oc", "qkgain", "windows", "w_oa", "w_o", "nffn", "w_r", "b_r",
           "w_gate", "b_gate", "w_up", "b_up", "w_down", "b_down"]


def kernel(**inputs):
    import concourse.bacc as _bacc
    import ml_dtypes
    from concourse.bass_utils import run_bass_kernel_spmd as _run

    arrays = {n: np.ascontiguousarray(a) for n, a in layout(inputs).items()}
    arrays["masks"] = window_masks().astype(ml_dtypes.bfloat16)
    nc = _bacc.Bacc("TRN2", target_bir_lowering=False, num_devices=1)
    aps = {n: nc.dram_tensor(f"in_{n}", arrays[n].shape, mybir.dt.from_np(arrays[n].dtype), kind="ExternalInput").ap()
           for n in _INPUTS + ["masks"]}
    out = nc.dram_tensor("out_rows", [ROWS_OUT, D], F32, kind="ExternalOutput").ap()
    build(nc, aps, out)
    r = _run(nc, [{f"in_{n}": arrays[n] for n in _INPUTS + ["masks"]}], core_ids=[0])
    return r.results[0]["out_rows"][:S].reshape(1, S, D)
```

```python
from contextlib import ExitStack

import numpy as np
import concourse.bass as bass
from concourse import mybir

F32 = mybir.dt.float32
F32R = mybir.dt.float32r
BF16 = mybir.dt.bfloat16
I32 = mybir.dt.int32
U32 = mybir.dt.uint32
ALU = mybir.AluOpType
ACT = mybir.ActivationFunctionType
AX = mybir.AxisListType

P = 128
D = 1024
S = 1024
KT = D // P
TT = S // P
CONV = 512
HEADS, HD = 8, 64
GRID_W, ROWS = 64, S // 64
WIN_R, WIN_C = 8, 16
QR, QC = 8, 16
KR, KC = 12, 32
KEYS = KR * KC
ROW_BASE = [0, 4]
COL_BASE = [0, 8, 24, 32]
COL_VAR = [0, 1, 1, 2]
BIG = 1e30
E, TOPK = 32, 4
SLOTS = 2 * P
MAX_PASSES = E + S * TOPK // SLOTS
NT = MAX_PASSES + 2
DUMMY = S
ROWS_OUT = S + SLOTS
EPS = 1e-6
LIMIT, ALPHA = 7.0, 1.702
FQ = 256
STEPS = 6
CH = 2048
NSLOT = 6
SPLIT = 4
POOL_LO = (5, 7, 9, 11)
HALVES = 13
ADDS = 6
MSLOT = 4
WIN = 15 * 63 + 48


def layout(np_inputs):
    a = {k: np.asarray(v) for k, v in np_inputs.items()}
    cols = lambda v: np.ascontiguousarray(v.reshape(-1, P).T)
    pad = np.zeros((HEADS, 23, 63), np.float32)
    pad[:, 4:19, 16:47] = a["rpb"][0]
    flat = pad.reshape(HEADS, -1)
    q = np.arange(P)
    start = (7 - q // QC) * 63 + 15 - q % QC
    windows = flat[:, start[:, None] + np.arange(WIN)[None, :]]
    return {
        "x": a["x"][0], "nmix": cols(a["norm_mix"][0]), "w_in": a["w_in"][0],
        "convw": np.ascontiguousarray(a["conv_w"][0].reshape(3, 4, P).transpose(2, 0, 1).reshape(P, 12)),
        "w_oc": a["w_out_conv"][0],
        "qkgain": np.stack([np.tile(a["k_norm"][0], 2), np.tile(a["q_norm"][0], 2)], 1),
        "windows": np.ascontiguousarray(windows), "w_oa": a["w_out_attn"][0], "w_o": a["w_o"][0],
        "nffn": a["norm_ffn"], "w_r": a["w_router"][0], "b_r": a["b_router"],
        "w_gate": a["w_gate"][0], "b_gate": a["b_gate"][0], "w_up": a["w_up"][0], "b_up": a["b_up"][0],
        "w_down": a["w_down"][0], "b_down": a["b_down"][0],
    }


def window_masks():
    out = np.zeros((P, 2, 3, KR, KC), np.float32)
    q = np.arange(P)
    for rb in range(2):
        r = 8 * rb + q // QC
        rs = np.clip(r - WIN_R // 2, 0, ROWS - WIN_R)
        kr = ROW_BASE[rb] + np.arange(KR)
        row_ok = (kr[None] >= rs[:, None]) & (kr[None] < rs[:, None] + WIN_R)
        for cb in (0, 1, 3):
            c = QC * cb + q % QC
            cs = np.clip(c - WIN_C // 2, 0, GRID_W - WIN_C)
            kc = COL_BASE[cb] + np.arange(KC)
            col_ok = (kc[None] >= cs[:, None]) & (kc[None] < cs[:, None] + WIN_C)
            ok = row_ok[:, :, None] & col_ok[:, None, :]
            out[:, rb, COL_VAR[cb]] = np.where(ok, 0.0, BIG)
    return out.reshape(P, 6 * KEYS)


def build(nc, A, out):
    ctx = ExitStack()
    with ctx:
        def sem(name):
            return ctx.enter_context(nc.semaphore(name))

        def sb(name, shape, dt=F32, where=ctx):
            return where.enter_context(nc.sbuf_tensor(name, shape, dt))

        bank = [ctx.enter_context(nc.psum_tensor(f"bank{i}", [P, 512], F32)) for i in range(8)]
        h2_rows = nc.dram_tensor("h2_rows", [ROWS_OUT, D], F32).ap()

        parts = ExitStack()
        ring_lo = sb("ring_lo", [P, NSLOT, CH], F32R, where=parts)
        parts.close()
        ring = sb("ring", [P, NSLOT, CH])
        ident = sb("ident", [P, P])
        ones_bf = sb("ones_bf", [P, P], BF16)
        tri_bf = sb("tri_bf", [P, P], BF16)
        ones_row = sb("ones_row", [1, P])
        br_row = sb("br_row", [1, E])
        wr = sb("wr", [P, KT, E])
        nmix = sb("nmix", [P, KT])
        convw = sb("convw", [P, 12])
        gain = sb("gain", [P, 2])
        ss = sb("ss", [P, TT])
        var = sb("var", [P, TT])
        rstd = sb("rstd", [P, TT])
        half = sb("half", [P, 8])
        logits = sb("logits", [P, TT, E])
        top_v = sb("top_v", [P, TT, 8])
        top_i = sb("top_i", [P, TT, 8], U32)
        iota_f = sb("iota_f", [P, SLOTS])
        iota_bf = sb("iota_bf", [P, SLOTS], BF16)
        dum_i = sb("dum_i", [P, 2], I32)
        dum = sb("dum", [P, 2])
        rows_bf = sb("rows_bf", [P, TT, E, 6], BF16)
        slot_of = sb("slot_of", [P, TT, E])
        table = sb("table", [1, 3 * NT + 1], I32)

        mix = ExitStack()
        hT = sb("hT", [P, KT, S], where=mix)
        qkT = sb("qkT", [P, 8, S], where=mix)
        vb = sb("vb", [P, 4, 4, CONV], where=mix)
        ypre = sb("ypre", [P, 4, S], where=mix)
        oT = sb("oT", [P, 4, S], where=mix)
        masks = sb("masks", [P, 6, KEYS], BF16, where=mix)
        bias = sb("bias", [P, 6, KEYS], where=mix)
        win = sb("win", [P, 16, 63], where=mix)
        ra, rb_ = ring[:, MSLOT, :], ring[:, MSLOT + 1, :]
        ss8 = sb("ss8", [P, 2, 8], where=mix)
        var8 = sb("var8", [P, 2, 8], where=mix)
        rs8 = sb("rs8", [P, 2, 8], where=mix)
        nmin = sb("nmin", [P, 2], where=mix)
        rsum = sb("rsum", [P, 2], where=mix)
        rinv = sb("rinv", [P, 2], where=mix)
        iota_i, ctile_i, cpart_i = (ypre[:, i, 0:SLOTS].bitcast(I32) for i in range(3))
        mixedT = qkT
        vnat = oT[:, :, :].rearrange("p a (b n) -> p (a b) n", b=2)
        xt = [ra[:, 0:1024], ra[:, 1024:2048]]
        junk = rb_[:, 0:1024]
        sq = rb_[:, 0:512]
        qn = [rb_[:, 512:1024], rb_[:, 1024:1536]]
        prob = [rb_[:, 0:384], rb_[:, 384:768]]
        probT = [rb_[:, 768:1152], rb_[:, 1152:1536]]
        u = [ra[:, 0:1024], ra[:, 1024:2048]]
        tmp = [ra[:, 512 * i:512 * i + 512] for i in range(4)]
        xe = [rb_[:, 0:1024], rb_[:, 1024:2048]]
        xn = [ra[:, 0:1024], ra[:, 1024:2048]]
        h2T = [hT[:, 0, :].rearrange("p (k t) -> p k t", k=KT), hT[:, 1, :].rearrange("p (k t) -> p k t", k=KT)]
        junk_e = hT[:, 2, :]
        gain_row = hT[:, 3, :]
        mix.close()

        gates = ExitStack()
        h_lo = sb("h_lo", [P, KT, S], F32R, where=gates)
        sb("qkT_place", [P, 8, S], where=gates)
        h_hi = sb("h_hi", [P, KT, S], F32R, where=gates)
        sb("ypre_oT_place", [P, 8, S], where=gates)
        sb("masks_place", [P, 6, KEYS], BF16, where=gates)
        gate_hi = sb("gate_hi", [P, 2 * D], F32R, where=gates)
        gates.close()

        moe = ExitStack()
        xg = [sb(f"xg{b}", [P, D], where=moe) for b in range(2)]
        xT = [[sb(f"xT{b}{h}", [P, KT, P], F32R, where=moe) for h in ("hi", "lo")] for b in range(2)]
        aT = [[sb(f"aT{b}{h}", [P, KT, P], F32R, where=moe) for h in ("hi", "lo")] for b in range(2)]
        gu = [sb(f"gu{b}", [P, 2 * FQ], where=moe) for b in range(2)]
        sg = [sb(f"sg{b}", [P, FQ], where=moe) for b in range(2)]
        act = [sb(f"act{b}", [P, FQ], where=moe) for b in range(2)]
        ys = [sb(f"ys{b}", [P, D], where=moe) for b in range(2)]
        brow = sb("brow", [1, 3 * D], where=moe)
        bbc = sb("bbc", [P, 3 * D], where=moe)
        pick = sb("pick", [P, TT, SLOTS], BF16, where=moe)
        slot_col = sb("slot_col", [P, TT, 1], where=moe)
        base = sb("base", [P, 1], where=moe)
        islot = sb("islot", [P, 12], where=moe)
        itmp = sb("itmp", [P, 3, 2], where=moe)
        idx_next = sb("idx_next", [P, 2], U32, where=moe)
        idx_cur = sb("idx_cur", [P, 2], U32, where=moe)
        gate_next = sb("gate_next", [P, 2], where=moe)
        gate_cur = sb("gate_cur", [P, 2], where=moe)
        gsum = sb("gsum", [P, 2], where=moe)
        warm = sb("warm", [P, 1], where=moe)
        route = ExitStack()
        rt = sb("rt", [P, 5, TT * E], where=route)
        oh = sb("oh", [P, TT * TOPK, E], where=route)
        ohg = sb("ohg", [P, TT * TOPK, E], where=route)
        topi_f = sb("topi_f", [P, TT, TOPK], where=route)
        ev = sb("ev", [P, TT, TOPK], where=route)
        gk = sb("gk", [P, TT, TOPK], where=route)
        esum = sb("esum", [P, TT], where=route)
        routed_bf = sb("routed_bf", [P, TT * E], BF16, where=route)
        before = sb("before", [P, TT + 1, E], where=route)
        npass = sb("npass", [P, E], where=route)
        scan = sb("scan", [P, 2, 16 + E], where=route)
        pexc = sb("pexc", [P, E], where=route)
        pass_e = sb("pass_e", [P, 4, E], where=route)
        pass_c = sb("pass_c", [P, 8], where=route)
        b_bf = sb("b_bf", [P, 1], BF16, where=route)
        b_row = sb("b_row", [1, NT], where=route)
        route.close()
        w_hi = sb("w_hi", [P, SPLIT, CH], F32R, where=moe)
        w_lo = sb("w_lo", [P, SPLIT, CH], F32R, where=moe)
        moe.close()

        consts_in = sem("consts_in")
        made = sem("made")
        pool_c = sem("pool_c")
        zero_out = sem("zero_out")
        x_in = [sem(f"x_in{i}") for i in range(2)]
        w_in = [sem(f"w_in{i}") for i in range(MSLOT)]
        w_used = sem("w_used")
        xsq = sem("xsq"); xvar = sem("xvar"); xrs = sem("xrs"); xnorm = sem("xnorm")
        xtr = sem("xtr"); xev = sem("xev")
        proj = sem("proj")
        qsq = sem("qsq"); qred = sem("qred"); qvar = sem("qvar"); qrs = sem("qrs"); qnorm = sem("qnorm"); qtr = sem("qtr"); qev = sem("qev")
        gain_ok = sem("gain_ok"); gain_in = sem("gain_in")
        vev = sem("vev"); v_moved = sem("v_moved")
        win_in = sem("win_in"); bias_ok = sem("bias_ok")
        sc = sem("sc"); smin = sem("smin"); sexp = sem("sexp"); sinv = sem("sinv"); snorm = sem("snorm")
        ptr = sem("ptr"); pev = sem("pev"); pvd = sem("pvd"); oev = sem("oev")
        uev = sem("uev"); cmul = sem("cmul"); cconv = sem("cconv"); bmul = sem("bmul")
        mtile = sem("mtile"); msig = sem("msig"); h_hi_ok = sem("h_hi_ok"); h_lo_ok = sem("h_lo_ok"); gate_hi_ok = sem("gate_hi_ok"); gate_lo_ok = sem("gate_lo_ok"); mmul = sem("mmul"); mixd = sem("mixd")
        e_mm = sem("e_mm"); xe_in = [sem(f"xe_in{i}") for i in range(2)]; e_x1 = sem("e_x1"); e_sq = sem("e_sq"); e_var = sem("e_var"); e_rs = sem("e_rs")
        e_xn = sem("e_xn"); e_tr = sem("e_tr"); e_ht = sem("e_ht"); e_lg = sem("e_lg"); e_lc = sem("e_lc"); e_mx = sem("e_mx"); e_ix = sem("e_ix")
        x1_out = [sem(f"x1_out{i}") for i in range(2)]; h2_out = [sem(f"h2_out{i}") for i in range(2)]
        f_dve = sem("f_dve"); f_dv = sem("f_dv"); f_exp = sem("f_exp"); f_pe = sem("f_pe"); f_bf = sem("f_bf"); f_col = sem("f_col"); f_row = sem("f_row"); f_done = sem("f_done"); table_ok = sem("table_ok")

        g_w = [sem(f"g_w{i}") for i in range(NSLOT)]
        g_warm = sem("g_warm"); g_hi = sem("g_hi"); g_lo = sem("g_lo"); g_plo = sem("g_plo")
        g_half = [sem(f"g_half{b}") for b in range(2)]
        g_add = [sem(f"g_add{b}") for b in range(2)]
        g_clip = [sem(f"g_clip{b}") for b in range(2)]
        g_sig = [sem(f"g_sig{b}") for b in range(2)]
        g_m1 = [sem(f"g_m1{b}") for b in range(2)]
        g_act = [sem(f"g_act{b}") for b in range(2)]
        g_atr = [sem(f"g_atr{b}") for b in range(2)]
        g_aev = [sem(f"g_aev{b}") for b in range(2)]
        g_alo = [sem(f"g_alo{b}") for b in range(2)]
        g_xhi = [sem(f"g_xhi{b}") for b in range(2)]
        g_ys = [sem(f"g_ys{b}") for b in range(2)]
        g_sc = [sem(f"g_sc{b}") for b in range(2)]
        g_pick = sem("g_pick"); g_imm = sem("g_imm"); g_ich = sem("g_ich"); g_idx = sem("g_idx"); g_cur = sem("g_cur")
        held = sem("held")
        g_added = sem("g_added"); g_base = sem("g_base"); g_col = sem("g_col")
        g_gat = [sem(f"g_gat{b}") for b in range(2)]
        g_xtr = [sem(f"g_xtr{b}") for b in range(2)]
        g_xev = [sem(f"g_xev{b}") for b in range(2)]
        g_brow = sem("g_brow"); g_bgu = sem("g_bgu"); g_bd = sem("g_bd")

        items = []
        wk = A["w_in"].rearrange("(k p) n -> p k n", p=P)
        for c0 in (2048, 1536, 2560):
            for kh in range(2):
                items.append([(wk[:, 4 * kh:4 * kh + 4, c0:c0 + 512], 0, 4, 512)])
        for j in range(4):
            items.append([(wk[:, :, P * j:P * j + P], 0, 8, P), (wk[:, :, 1024 + P * j:1024 + P * j + P], 1024, 8, P)])
            items.append([(wk[:, :, 512 + P * j:512 + P * j + P], 0, 8, P)])
        woc = A["w_oc"].rearrange("(k p) n -> p k n", p=P)
        woa = A["w_oa"].rearrange("(k p) n -> p k n", p=P)
        for d in range(8):
            items.append([(wk[:, :, 3072 + P * d:3072 + P * d + P], 0, 8, P), (wk[:, :, 4096 + P * d:4096 + P * d + P], 1024, 8, P)])
            items.append([(woc[:, :, P * d:P * d + P], 0, 4, P), (woa[:, :, P * d:P * d + P], 512, 4, P)])
        wo = A["w_o"].rearrange("(k p) n -> p k n", p=P)
        for k2 in range(4):
            items.append([(wo[:, 2 * k2:2 * k2 + 2, :], 0, 2, D)])
        NI = len(items)
        landed, total = [], [0] * MSLOT
        for n, it in enumerate(items):
            total[n % MSLOT] += 16 * len(it)
            landed.append(total[n % MSLOT])
        IT_CONV, IT_MERGE, IT_WO = 6, 14, 30

        def item_view(n, off, k, w):
            return ring[:, n % MSLOT, off:off + k * w].rearrange("p (k n) -> p k n", k=k)

        def wait_item(e, n):
            e.wait_ge(w_in[n % MSLOT], landed[n])

        NCONST = 7
        units = HEADS * 8
        unit_end = [(m + 1) * units // 24 for m in range(24)]

        def unit(n):
            h, b = n // 8, n % 8
            rb, cb = b // 4, b % 4
            return h, rb, cb, 3 * rb + COL_VAR[cb]

        def q_evacs(n):
            return n + max(0, n - TT)
        LAST_USE = [0, 2, 3, 4, 6, 7]

        def halves(c):
            return c + 1 if c < 11 else HALVES

        def wait_lo(wait, p, c):
            if c in POOL_LO:
                wait(g_plo, 1 + len(POOL_LO) * p + POOL_LO.index(c) + 1)
            else:
                n = len(POOL_LO)
                wait(g_lo, 1 + (12 - n) * p + c + 1 - sum(i < c for i in POOL_LO))

        def hold(e, s, value):
            e.wait_ge(s, value)
            e.sem_inc(held, 1)

        block = ctx.enter_context(nc.Block())

        @block.sync
        def _(e):
            for dst, src in ((nmix[:, :], A["nmix"]), (convw[:, :], A["convw"]),
                             (gain[:, :], A["qkgain"]), (br_row[:, :], A["b_r"]),
                             (wr[:, :, :], A["w_r"].rearrange("(k p) n -> p k n", p=P)),
                             (masks[:, :, :], A["masks"].rearrange("p (v n) -> p v n", v=6))):
                e.dma_start(dst, src).then_inc(consts_in, 16)
            e.dma_start(xt[0], A["x"][0:P, :]).then_inc(x_in[0], 16)
            e.dma_start(xt[1], A["x"][P:2 * P, :]).then_inc(x_in[1], 16)

            def load_item(n):
                if n >= MSLOT:
                    e.wait_ge(w_used, n - MSLOT + 1)
                for src, off, k, w in items[n]:
                    e.dma_start(item_view(n, off, k, w), src).then_inc(w_in[n % MSLOT], 16)
            load_item(0)
            load_item(1)
            for t in range(2, TT):
                e.wait_ge(xtr, t - 1)
                e.dma_start(xt[t % 2], A["x"][P * t:P * t + P, :]).then_inc(x_in[t % 2], 16)
            for n in range(2, 6):
                load_item(n)
            e.wait_ge(made, 2)
            for dst in (out, h2_rows):
                for r in (S, S + P):
                    e.dma_start(dst[r:r + P, :], oT[:, 0, :]).then_inc(zero_out, 16)
            for n in range(6, 10):
                load_item(n)
            e.wait_ge(vev, TT)
            for cb in range(4):
                for i in range(4):
                    p0 = 64 * (i % 2) + COL_BASE[cb]
                    e.dma_start(vb[32 * i:32 * i + 32, cb, :, :], vnat[p0:p0 + 32, i // 2:TT:2, :]).then_inc(v_moved, 16)
            for n in range(10, NI):
                load_item(n)
            for t in range(TT):
                if t == 0:
                    e.wait_ge(oev, units)
                    e.wait_ge(mixd, 16)
                    e.dma_start(gain_row, A["nffn"].to_broadcast([P, D])).then_inc(gain_in, 16)
                    e.dma_start(xe[0], A["x"][0:P, :]).then_inc(xe_in[0], 16)
                    e.dma_start(xe[1], A["x"][P:2 * P, :]).then_inc(xe_in[1], 16)
                e.wait_ge(e_x1, 2 * t + 2)
                e.dma_start(out[P * t:P * t + P, :], xe[t % 2]).then_inc(x1_out[t % 2], 16)
                e.wait_ge(e_xn, t + 1)
                e.dma_start(h2_rows[P * t:P * t + P, :], xn[t % 2]).then_inc(h2_out[t % 2], 16)
                if t + 2 < TT:
                    e.wait_ge(x1_out[t % 2], 16 * (t // 2 + 1))
                    e.dma_start(xe[t % 2], A["x"][P * (t + 2):P * (t + 3), :]).then_inc(xe_in[t % 2], 16)

            wg = A["w_gate"].rearrange("e (k p) n -> p e k n", p=P)
            wu = A["w_up"].rearrange("e (k p) n -> p e k n", p=P)
            wd = A["w_down"].rearrange("e (k p) n -> p e k n", p=P)

            def load_half_step(c, ex):
                s, kh = c // 2, c % 2
                view = ring[:, c % NSLOT, :].rearrange("p (k n) -> p k n", k=4)
                if s < 4:
                    for j, w in enumerate((wg, wu)):
                        src = w[:, bass.ds(ex, 1), 4 * kh:4 * kh + 4, FQ * s:FQ * s + FQ].rearrange("p e k n -> p (e k) n")
                        e.dma_start(view[:, :, FQ * j:FQ * j + FQ], src).then_inc(g_w[c % NSLOT], 16)
                else:
                    for j in range(2):
                        src = wd[:, bass.ds(ex, 1), 2 * (c - 8) + j:2 * (c - 8) + j + 1, :].rearrange("p e k n -> p (e k n)")
                        e.dma_start(ring[:, c % NSLOT, D * j:D * j + D], src).then_inc(g_w[c % NSLOT], 16)

            def load_bias_rows(ex):
                for j, b in enumerate((A["b_gate"], A["b_up"])):
                    e.dma_start(brow[0:1, 0:2 * D].rearrange("o (s j n) -> o s j n", s=4, j=2)[:, :, j, :],
                                b[bass.ds(ex, 1), :].rearrange("o (s n) -> o s n", s=4)).then_inc(g_brow, 16)
                e.dma_start(brow[0:1, 2 * D:3 * D], A["b_down"][bass.ds(ex, 1), :]).then_inc(g_brow, 16)
            e.wait_ge(w_used, NI)
            e.wait_ge(table_ok, 1)
            n_pass = e.value_load(table[0:1, 3 * NT:3 * NT + 1], min_val=1, max_val=MAX_PASSES)
            ex0 = e.value_load(table[0:1, 0:1], min_val=0, max_val=E - 1)
            for c in range(NSLOT):
                load_half_step(c, ex0)
            load_bias_rows(ex0)
            with e.Fori(0, n_pass) as p:
                ex = e.value_load(table[0:1, bass.ds(p, 1)], min_val=0, max_val=E - 1)
                exn = e.value_load(table[0:1, bass.ds(p + 1, 1)], min_val=0, max_val=E - 1)
                for c in range(NSLOT, 12):
                    wait_lo(lambda s, v: hold(e, s, v), p, c - NSLOT)
                    load_half_step(c, ex)
                hold(e, g_bgu, 1 + p + 1)
                hold(e, g_bd, 1 + p + 1)
                load_bias_rows(exn)
                with e.If(p + 1 < n_pass):
                    for c in range(NSLOT):
                        wait_lo(lambda s, v: hold(e, s, v), p, c + NSLOT)
                        load_half_step(c, exn)
            e.wait_ge(zero_out, 64)
            e.wait_ge(x1_out[0], 16 * TT // 2)
            e.wait_ge(x1_out[1], 16 * TT // 2)

        @block.gpsimd
        def _(e):
            for s in (g_plo, g_bgu, g_bd):
                e.sem_inc(s, 1)
            e.memset(ident[:, :], 0.0).then_inc(pool_c, 1)
            e.memset(tri_bf[:, :], 1.0).then_inc(pool_c, 1)
            e.memset(ones_bf[:, :], 1.0).then_inc(pool_c, 1)
            e.memset(ones_row[:, :], 1.0).then_inc(pool_c, 1)
            e.memset(half[:, :], -0.5).then_inc(pool_c, 1)
            e.iota(iota_i, pattern=[[1, SLOTS]], base=0, channel_multiplier=0).then_inc(pool_c, 1)
            e.iota(ctile_i, pattern=[[P, TT], [0, E]], base=0, channel_multiplier=0).then_inc(pool_c, 1)
            e.iota(cpart_i, pattern=[[0, TT * E]], base=0, channel_multiplier=1).then_inc(pool_c, 1)
            e.iota(dum_i[:, :], pattern=[[P, 2]], base=DUMMY, channel_multiplier=1).then_inc(pool_c, 1)
            e.wait_ge(pool_c, 9)
            e.affine_select(out=ident[:, :], in_=ident[:, :], compare_op=ALU.not_equal, fill=1.0,
                            base=0, pattern=[[-1, P]], channel_multiplier=1).then_inc(made, 1)
            e.memset(oT[:, 0, :], 0.0).then_inc(made, 1)
            e.affine_select(out=tri_bf[:, :], in_=tri_bf[:, :], compare_op=ALU.is_ge, fill=0.0,
                            base=0, pattern=[[1, P]], channel_multiplier=-1).then_inc(made, 1)
            e.tensor_copy(iota_f[:, :], iota_i).then_inc(made, 1)
            e.tensor_copy(iota_bf[:, :], iota_i).then_inc(made, 1)
            e.tensor_copy(dum[:, :], dum_i[:, :]).then_inc(made, 1)
            r2 = rows_bf[:, :, :, :].rearrange("p t e c -> p (t e) c")
            e.tensor_copy(r2[:, :, 0], ctile_i).then_inc(made, 1)
            e.tensor_copy(r2[:, :, 1], cpart_i).then_inc(made, 1)
            e.memset(r2[:, :, 2], 1.0).then_inc(made, 1)

            for t in range(TT):
                e.wait_ge(xvar, t + 1)
                e.tensor_tensor(rstd[:, t:t + 1], var[:, t:t + 1], half[:, 0:1], ALU.pow).then_inc(xrs, 1)
            for n in range(2 * TT):
                e.wait_ge(qvar, n + 1)
                if n >= 2:
                    e.wait_ge(qnorm, n - 1)
                e.tensor_tensor(rs8[:, n % 2, :], var8[:, n % 2, :], half[:, :], ALU.pow).then_inc(qrs, 1)
            e.wait_ge(consts_in, 16 * (NCONST - 1))
            for h in range(HEADS):
                if h:
                    e.wait_ge(bias_ok, 6 * h)
                e.dma_start(win[:, :, :].rearrange("p r c -> p (r c)")[:, 0:WIN], A["windows"][h, :, :]).then_inc(win_in, 16)
                e.wait_ge(win_in, 16 * (h + 1))
                for v in range(6):
                    rb, cv = v // 3, v % 3
                    r0, c0 = (4, 0)[rb], (16, 8, 0)[cv]
                    if h:
                        e.wait_ge(smin, 8 * (h - 1) + LAST_USE[v] + 1)
                    e.tensor_tensor(bias[:, v, :].rearrange("p (r c) -> p r c", r=KR),
                                    masks[:, v, :].rearrange("p (r c) -> p r c", r=KR),
                                    win[:, r0:r0 + KR, c0:c0 + KC], ALU.subtract).then_inc(bias_ok, 1)
            for t in range(TT):
                e.wait_ge(e_var, t + 1)
                e.tensor_tensor(rstd[:, t:t + 1], var[:, t:t + 1], half[:, 0:1], ALU.pow).then_inc(e_rs, 1)

            e.wait_ge(table_ok, 1)
            e.wait_ge(h2_out[0], 16 * TT // 2)
            e.wait_ge(h2_out[1], 16 * TT // 2)
            e.wait_ge(zero_out, 64)
            e.wait_ge(x1_out[0], 16 * TT // 2)
            e.wait_ge(x1_out[1], 16 * TT // 2)
            n_pass = e.value_load(table[0:1, 3 * NT:3 * NT + 1], min_val=1, max_val=MAX_PASSES)

            def expert_of(n):
                return (e.value_load(table[0:1, bass.ds(n, 1)], min_val=0, max_val=E - 1),
                        e.value_load(table[0:1, bass.ds(n + NT, 1)], min_val=0, max_val=1),
                        e.value_load(table[0:1, bass.ds(n + 2 * NT, 1)], min_val=0, max_val=MAX_PASSES))

            def rest_of_weights(c, p):
                hold(e, g_hi, 1 + 12 * p + c + 1)
                e.tensor_tensor(w_lo[:, c % SPLIT, :], ring[:, c % NSLOT, :], w_hi[:, c % SPLIT, :].bitcast(F32), ALU.subtract).then_inc(g_plo, 1)

            def gather(n, hb):
                hold(e, g_idx, 1 + 2 * n + 2)
                hold(e, g_xtr[0], 1 + n)
                e.indirect_dma_start(out=xg[0][:, :], out_offset=None, in_=h2_rows,
                                     in_offset=bass.IndirectOffsetOnAxis(ap=idx_next[:, 0:1], axis=0)).then_inc(g_gat[0], 16)
                with e.If(hb > 0):
                    e.indirect_dma_start(out=xg[1][:, :], out_offset=None, in_=h2_rows,
                                         in_offset=bass.IndirectOffsetOnAxis(ap=idx_next[:, 1:2], axis=0)).then_inc(g_gat[1], 16)

            ex, hb, nb = expert_of(0)
            gather(0, hb)
            e.wait_ge(g_brow, 48)
            e.partition_broadcast(bbc[:, 0:2 * D], brow[0:1, 0:2 * D]).then_inc(g_bgu, 1)
            e.partition_broadcast(bbc[:, 2 * D:3 * D], brow[0:1, 2 * D:3 * D]).then_inc(g_bd, 1)

            with e.Fori(0, n_pass) as p:
                _, hb, nb = expert_of(p)
                exn, hbn, nbn = expert_of(p + 1)

                rest_of_weights(POOL_LO[0], p)
                with e.If(p > 0):
                    hold(e, g_sc[0], 16 * p)
                with e.If(nb > 0):
                    hold(e, g_sc[1], 16 * nb)
                e.sem_inc(g_added, 1)
                rest_of_weights(POOL_LO[1], p)
                hold(e, g_xtr[1], 1 + nb + hb)
                gather(p + 1, hbn)
                rest_of_weights(POOL_LO[2], p)
                hold(e, g_brow, 48 * p + 96)
                hold(e, g_add[0], 2 + ADDS * p + 4)
                hold(e, g_add[1], 2 + ADDS * nb + 4 * hb)
                e.partition_broadcast(bbc[:, 0:2 * D], brow[0:1, 0:2 * D]).then_inc(g_bgu, 1)
                rest_of_weights(POOL_LO[3], p)
                hold(e, g_ys[0], 1 + 2 * p + 2)
                e.indirect_dma_start(out=out, out_offset=bass.IndirectOffsetOnAxis(ap=idx_cur[:, 0:1], axis=0),
                                     in_=ys[0][:, :], in_offset=None, compute_op=ALU.add).then_inc(g_sc[0], 16)
                with e.If(hb > 0):
                    hold(e, g_ys[1], 1 + 2 * nb + 2)
                    e.indirect_dma_start(out=out, out_offset=bass.IndirectOffsetOnAxis(ap=idx_cur[:, 1:2], axis=0),
                                         in_=ys[1][:, :], in_offset=None, compute_op=ALU.add).then_inc(g_sc[1], 16)
                hold(e, g_add[0], 2 + ADDS * p + ADDS)
                hold(e, g_add[1], 2 + ADDS * (nb + hb))
                e.partition_broadcast(bbc[:, 2 * D:3 * D], brow[0:1, 2 * D:3 * D]).then_inc(g_bd, 1)
            b_total = e.value_load(table[0:1, bass.ds(n_pass + 2 * NT, 1)], min_val=0, max_val=MAX_PASSES)
            hold(e, g_sc[0], 16 * n_pass)
            with e.If(b_total > 0):
                hold(e, g_sc[1], 16 * b_total)

        @block.scalar
        def _(e):
            for s in (g_warm, g_hi, *g_sig, *g_aev, *g_xhi, *g_ys):
                e.sem_inc(s, 1)
            for t in range(TT):
                e.wait_ge(x_in[t % 2], 16 * (t // 2 + 1))
                if t:
                    e.wait_ge(xsq, t)
                e.activation(junk, xt[t % 2], ACT.Square, accum_out=ss[:, t:t + 1]).then_inc(xsq, 1)
            e.wait_ge(gain_ok, 1)

            def squares(n):
                e.wait_ge(proj, n + 1)
                if n:
                    e.wait_ge(qred, n)
                e.activation(sq, bank[n % 2][:, :], ACT.Square).then_inc(qsq, 1)

            def transposed(n):
                e.wait_ge(qtr, n + 1)
                g, t = n // TT, n % TT
                src = bank[2 + n % 2][:, :].rearrange("p (h t) -> p h t", h=4)
                if g == 0:
                    e.activation(qkT[:, 0:4, P * t:P * t + P], src, ACT.Copy, scale=gain[:, 0:1]).then_inc(qev, 1)
                else:
                    for i in range(2):
                        rb, r = (2 * t + i) // QR, (2 * t + i) % QR
                        dst = qkT[:, 4:8, 512 * rb:512 * rb + 512].rearrange("p h (b q) -> p h b q", b=4)[:, :, :, QC * r:QC * r + QC]
                        ins = e.activation(dst, src[:, :, GRID_W * i:GRID_W * i + GRID_W].rearrange("p h (b c) -> p h b c", b=4),
                                           ACT.Copy, scale=gain[:, 1:2])
                        ins.then_inc(qev, 1)

            for n in range(2 * TT):
                squares(n)
                if n:
                    transposed(n - 1)
            for t in range(TT):
                n = 2 * TT + t
                e.wait_ge(proj, n + 1)
                if t == 0:
                    e.wait_ge(zero_out, 64)
                e.activation(vnat[:, t, :], bank[n % 2][:, :], ACT.Copy).then_inc(vev, 1)
                if t == 0:
                    transposed(n - 1)

            def exps(n):
                e.wait_ge(smin, n + 1)
                e.activation(prob[n % 2], prob[n % 2], ACT.Exp, bias=nmin[:, n % 2:n % 2 + 1], scale=-1.0,
                             accum_out=rsum[:, n % 2:n % 2 + 1]).then_inc(sexp, 1)

            def probs_out(n):
                e.wait_ge(ptr, n + 1)
                if n >= 2:
                    e.wait_ge(pvd, n - 1)
                e.activation(probT[n % 2], bank[4 + n % 2][:, 0:KEYS], ACT.Copy).then_inc(pev, 1)
            un = 0
            for m in range(24):
                j, part, hf = m // 6, (m % 6) // 2, m % 2
                if part == 0:
                    e.wait_ge(proj, 3 * TT + m + 1)
                    if j >= 2:
                        e.wait_ge(cconv, j - 1)
                    e.activation(u[j % 2][:, 512 * hf:512 * hf + 512], bank[m % 2][:, :], ACT.Copy).then_inc(uev, 1)
                while un < unit_end[m]:
                    exps(un)
                    if un:
                        probs_out(un - 1)
                    un += 1
            probs_out(units - 1)

            def round_gate_weights(d):
                wait_item(e, IT_MERGE + 2 * d)
                if d:
                    e.wait_ge(mtile, 8 * d)
                e.activation(gate_hi[:, :], ring[:, (IT_MERGE + 2 * d) % MSLOT, :], ACT.Copy).then_inc(gate_hi_ok, 1)
            round_gate_weights(0)
            e.wait_ge(oev, units)
            for k in range(KT):
                e.activation(h_hi[:, k, :], hT[:, k, :], ACT.Copy).then_inc(h_hi_ok, 1)
            for n in range(16):
                for g in range(2):
                    e.wait_ge(mtile, 4 * n + 2 + g + 1)
                    if n == 0 and g == 0:
                        e.wait_ge(bmul, 8)
                    if n:
                        e.wait_ge(mmul, 2 * (n - 1) + g + 1)
                    e.activation(tmp[g], bank[4 * (n % 2) + g][:, :], ACT.Sigmoid).then_inc(msig, 1)
                if n % 2 == 1 and n < 15:
                    round_gate_weights(n // 2 + 1)
            for t in range(TT):
                e.wait_ge(e_x1, 2 * t + 2)
                if t:
                    e.wait_ge(e_sq, t)
                e.activation(junk_e, xe[t % 2], ACT.Square, accum_out=ss[:, t:t + 1]).then_inc(e_sq, 1)
            e.wait_ge(f_dv, 1)
            e.activation(ev[:, :, :], ev[:, :, :], ACT.Exp).then_inc(f_exp, 1)

            e.wait_ge(table_ok, 1)
            n_pass = e.value_load(table[0:1, 3 * NT:3 * NT + 1], min_val=1, max_val=MAX_PASSES)

            def round_weights(c, p, after):
                if after:
                    for b in range(2):
                        e.wait_ge(g_half[b], after[b])
                slot = c % NSLOT
                e.wait_ge(g_w[slot], 64 * p + 32 * (c // NSLOT) + 32)
                e.activation(w_hi[:, c % SPLIT, :], ring[:, slot, :], ACT.Copy).then_inc(g_hi, 1)

            def round_rows(b, at):
                e.wait_ge(g_xtr[b], 1 + at + 1)
                for i in range(2):
                    e.activation(xT[b][0][:, 4 * i:4 * i + 4, :], bank[4 + i][:, :].rearrange("p (k t) -> p k t", k=4), ACT.Copy).then_inc(g_xhi[b], 1)
            e.wait_ge(f_done, 1)
            for c in range(SPLIT):
                round_weights(c, 0, None)
            round_rows(0, 0)
            hb0 = e.value_load(table[0:1, NT:NT + 1], min_val=0, max_val=1)
            with e.If(hb0 > 0):
                round_rows(1, 0)
            with e.Fori(0, n_pass) as p:
                hb = e.value_load(table[0:1, bass.ds(p + NT, 1)], min_val=0, max_val=1)
                nb = e.value_load(table[0:1, bass.ds(p + 2 * NT, 1)], min_val=0, max_val=MAX_PASSES)
                hbn = e.value_load(table[0:1, bass.ds(p + 1 + NT, 1)], min_val=0, max_val=1)

                e.wait_ge(g_warm, 1 + p)
                e.activation(warm[:, :], half[:, 0:1], ACT.Sigmoid).then_inc(g_warm, 1)

                def sigmoid(b, s, at):
                    e.wait_ge(g_clip[b], 1 + 8 * at + 2 * s + 1)
                    e.activation(sg[b][:, :], gu[b][:, 0:FQ], ACT.Sigmoid, scale=ALPHA).then_inc(g_sig[b], 1)

                def act_out(b, s, at):
                    e.wait_ge(g_atr[b], 1 + 4 * at + s + 1)
                    e.activation(aT[b][0][:, 2 * s:2 * s + 2, :], bank[6 + b][:, 0:FQ].rearrange("p (k t) -> p k t", k=2),
                                 ACT.Copy).then_inc(g_aev[b], 1)

                def y_out(b, h, at):
                    e.wait_ge(g_add[b], 2 + ADDS * at + 4 + h + 1)
                    e.activation(ys[b][:, 512 * h:512 * h + 512], ys[b][:, 512 * h:512 * h + 512], ACT.Copy, scale=gate_cur[:, b:b + 1]).then_inc(g_ys[b], 1)

                def weights(c):
                    n = halves(c - SPLIT)
                    after = (1 + HALVES * p + n, 1 + HALVES * nb + hb * n)
                    if c < 12:
                        round_weights(c, p, after)
                    else:
                        with e.If(p + 1 < n_pass):
                            round_weights(c - 12, p + 1, after)

                for s in range(STEPS):
                    weights(2 * s + 4)
                    if s == 4:
                        round_rows(0, p + 1)
                    if s == 5:
                        with e.If(hbn > 0):
                            round_rows(1, nb + hb)
                    if s == 4:
                        act_out(0, 3, p)
                        with e.If(hb > 0):
                            act_out(1, 3, nb)
                    weights(2 * s + 5)
                    if s < 4:
                        sigmoid(0, s, p)
                        with e.If(hb > 0):
                            sigmoid(1, s, nb)
                    if 1 <= s <= 3:
                        act_out(0, s - 1, p)
                        with e.If(hb > 0):
                            act_out(1, s - 1, nb)
                for h in range(2):
                    y_out(0, h, p)
                with e.If(hb > 0):
                    for h in range(2):
                        y_out(1, h, nb)

        @block.vector
        def _(e):
            for s in (g_lo, g_pick, g_base, g_col, *g_add, *g_add, *g_clip, *g_m1, *g_act, *g_alo, *g_xev, g_ich, g_idx, g_cur):
                e.sem_inc(s, 1)
            e.wait_ge(consts_in, 16 * (NCONST - 1))
            e.tensor_scalar(gain[:, 1:2], gain[:, 1:2], -float(HD) ** -0.5, None, ALU.mult).then_inc(gain_ok, 1)

            def x_evac(t):
                e.wait_ge(xtr, t + 1)
                for i in range(2):
                    e.tensor_tensor(hT[:, 4 * i:4 * i + 4, P * t:P * t + P],
                                    bank[4 + 2 * (t % 2) + i][:, :].rearrange("p (k t) -> p k t", k=4),
                                    nmix[:, 4 * i:4 * i + 4, None].to_broadcast([P, 4, P]), ALU.mult).then_inc(xev, 1)
            for t in range(TT):
                e.wait_ge(xsq, t + 1)
                e.tensor_scalar(var[:, t:t + 1], ss[:, t:t + 1], 1.0 / D, EPS, ALU.mult, ALU.add).then_inc(xvar, 1)
                e.wait_ge(xrs, t + 1)
                e.tensor_scalar(xt[t % 2], xt[t % 2], rstd[:, t:t + 1], None, ALU.mult).then_inc(xnorm, 1)
                if t:
                    x_evac(t - 1)
            x_evac(TT - 1)
            for n in range(2 * TT):
                e.wait_ge(qsq, n + 1)
                e.tensor_reduce(ss8[:, n % 2, :], sq.rearrange("p (h d) -> p h d", h=HEADS), AX.X, ALU.add).then_inc(qred, 1)
                e.wait_ge(qred, n + 1)
                if n >= 2:
                    e.wait_ge(qrs, n - 1)
                e.tensor_scalar(var8[:, n % 2, :], ss8[:, n % 2, :], 1.0 / HD, EPS, ALU.mult, ALU.add).then_inc(qvar, 1)
                e.wait_ge(qrs, n + 1)
                if n >= 2:
                    e.wait_ge(qtr, n - 1)
                e.tensor_tensor(qn[n % 2].rearrange("p (h d) -> p h d", h=HEADS),
                                bank[n % 2][:, :].rearrange("p (h d) -> p h d", h=HEADS),
                                rs8[:, n % 2, :, None].to_broadcast([P, HEADS, HD]), ALU.mult).then_inc(qnorm, 1)

            def min_of(n):
                h, rb, cb, v = unit(n)
                e.wait_ge(sc, n + 1)
                e.wait_ge(bias_ok, 6 * h + v + 1)
                if n >= 2:
                    e.wait_ge(ptr, n - 1)
                if n == 0:
                    e.wait_ge(qtr, 2 * TT)
                e.tensor_tensor_reduce(out=prob[n % 2], in0=bank[2 + n % 2][:, 0:KEYS], in1=bias[:, v, :], scale=1.0,
                                       scalar=3.0e38, op0=ALU.add, op1=ALU.min, accum_out=nmin[:, n % 2:n % 2 + 1]).then_inc(smin, 1)

            def normalise(n):
                e.wait_ge(sexp, n + 1)
                e.reciprocal(rinv[:, n % 2:n % 2 + 1], rsum[:, n % 2:n % 2 + 1]).then_inc(sinv, 1)
                e.wait_ge(sinv, n + 1)
                e.tensor_scalar(prob[n % 2], prob[n % 2], rinv[:, n % 2:n % 2 + 1], None, ALU.mult).then_inc(snorm, 1)

            def attn_out(n):
                h, rb, cb, v = unit(n)
                e.wait_ge(pvd, n + 1)
                if n == 0:
                    e.wait_ge(v_moved, 256)
                h0 = HD * (h % 2)
                dst = oT[h0:h0 + HD, h // 2, :].rearrange("p (r c) -> p r c", c=GRID_W)
                e.tensor_copy(dst[:, QR * rb:QR * rb + QR, QC * cb:QC * cb + QC],
                              bank[6 + n % 2][h0:h0 + HD, 0:P].rearrange("p (r c) -> p r c", c=QC)).then_inc(oev, 1)
            un = 0
            for m in range(24):
                j, part, hf = m // 6, (m % 6) // 2, m % 2
                cols = slice(512 * hf, 512 * hf + 512)
                if part == 1:
                    e.wait_ge(proj, 3 * TT + m + 1)
                    e.wait_ge(uev, 2 * j + hf + 1)
                    e.tensor_tensor(u[j % 2][:, cols], bank[m % 2][:, :], u[j % 2][:, cols], ALU.mult).then_inc(cmul, 1)
                if part == 1 and hf == 1:
                    y, uu = ypre[:, j, :], u[j % 2]
                    e.wait_ge(cmul, 2 * j + 2)
                    e.tensor_scalar(y, uu, convw[:, 4 + j:5 + j], None, ALU.mult).then_inc(f_dve, 1)
                    e.wait_ge(f_dve, 2 * j + 1)
                    e.scalar_tensor_tensor(out=y[:, 1:S], in0=uu[:, 0:S - 1], scalar=convw[:, j:j + 1], in1=y[:, 1:S],
                                           op0=ALU.mult, op1=ALU.add).then_inc(f_dve, 1)
                    e.wait_ge(f_dve, 2 * j + 2)
                    e.scalar_tensor_tensor(out=y[:, 0:S - 1], in0=uu[:, 1:S], scalar=convw[:, 8 + j:9 + j], in1=y[:, 0:S - 1],
                                           op0=ALU.mult, op1=ALU.add).then_inc(cconv, 1)
                if part == 2:
                    e.wait_ge(proj, 3 * TT + m + 1)
                    e.wait_ge(cconv, j + 1)
                    e.tensor_tensor(ypre[:, j, cols], bank[m % 2][:, :], ypre[:, j, cols], ALU.mult).then_inc(bmul, 1)
                while un < unit_end[m]:
                    min_of(un)
                    if un >= 2:
                        attn_out(un - 2)
                    normalise(un)
                    un += 1
            attn_out(units - 2)
            attn_out(units - 1)

            def rest_of_gate_weights(d):
                e.wait_ge(gate_hi_ok, d + 1)
                slot = ring[:, (IT_MERGE + 2 * d) % MSLOT, :]
                e.tensor_tensor(ring_lo[:, (IT_MERGE + 2 * d) % MSLOT, :], slot, gate_hi[:, :].bitcast(F32), ALU.subtract).then_inc(gate_lo_ok, 1)
            rest_of_gate_weights(0)
            e.wait_ge(proj, 3 * TT + 24)
            for k in range(KT):
                e.wait_ge(h_hi_ok, k + 1)
                e.tensor_tensor(h_lo[:, k, :], hT[:, k, :], h_hi[:, k, :].bitcast(F32), ALU.subtract).then_inc(h_lo_ok, 1)
            for n in range(16):
                d, hf = n // 2, n % 2
                for g in range(2):
                    e.wait_ge(msig, 2 * n + g + 1)
                    e.wait_ge(mtile, 4 * n + g + 1)
                    if n:
                        e.wait_ge(mixd, n)
                    e.tensor_tensor(tmp[2 + g], bank[4 * (n % 2) + 2 + g][:, :], tmp[g], ALU.mult).then_inc(mmul, 1)
                e.wait_ge(mmul, 2 * n + 2)
                e.tensor_tensor(mixedT[:, d, 512 * hf:512 * hf + 512], tmp[2], tmp[3], ALU.add).then_inc(mixd, 1)
                if hf == 1 and d < 7:
                    rest_of_gate_weights(d + 1)

            def h2_evac(t):
                e.wait_ge(e_tr, t + 1)
                if t >= 2:
                    e.wait_ge(e_lg, t - 1)
                for i in range(2):
                    e.tensor_copy(h2T[t % 2][:, 4 * i:4 * i + 4, :],
                                  bank[4 + i][:, :].rearrange("p (k t) -> p k t", k=4)).then_inc(e_ht, 1)

            def top(t):
                e.wait_ge(e_lg, t + 1)
                e.tensor_copy(logits[:, t, :], bank[6 + t % 2][:, 0:E]).then_inc(e_lc, 1)
                e.wait_ge(e_lc, t + 1)
                e.max(out=top_v[:, t, :], in_=logits[:, t, :]).then_inc(e_mx, 1)
                e.wait_ge(e_mx, t + 1)
                e.max_index(out=top_i[:, t, :], in_max=top_v[:, t, :], in_values=logits[:, t, :]).then_inc(e_ix, 1)
            for t in range(TT):
                e.wait_ge(xe_in[t % 2], 16 * (t // 2 + 1))
                for i in range(2):
                    e.wait_ge(e_mm, 2 * t + i + 1)
                    e.tensor_tensor(xe[t % 2][:, 512 * i:512 * i + 512], bank[2 * (t % 2) + i][:, :],
                                    xe[t % 2][:, 512 * i:512 * i + 512], ALU.add).then_inc(e_x1, 1)
                e.wait_ge(e_sq, t + 1)
                e.tensor_scalar(var[:, t:t + 1], ss[:, t:t + 1], 1.0 / D, EPS, ALU.mult, ALU.add).then_inc(e_var, 1)
                e.wait_ge(e_rs, t + 1)
                if t >= 2:
                    e.wait_ge(h2_out[t % 2], 16 * (t // 2))
                    e.wait_ge(e_tr, t - 1)
                if t == 0:
                    e.wait_ge(gain_in, 16)
                e.scalar_tensor_tensor(out=xn[t % 2], in0=xe[t % 2], scalar=rstd[:, t:t + 1], in1=gain_row,
                                       op0=ALU.mult, op1=ALU.mult).then_inc(e_xn, 1)
                if t:
                    h2_evac(t - 1)
                if t >= 2:
                    top(t - 2)
            h2_evac(TT - 1)
            top(TT - 2)
            top(TT - 1)

            chain = [8]

            def link(ins):
                chain[0] += 1
                ins.then_inc(f_dve, 1)
                e.wait_ge(f_dve, chain[0])
            e.wait_ge(e_ix, TT)
            e.wait_ge(made, 9)
            e.wait_ge(h2_out[0], 16 * TT // 2)
            e.wait_ge(h2_out[1], 16 * TT // 2)
            e.wait_ge(x1_out[0], 16 * TT // 2)
            e.wait_ge(x1_out[1], 16 * TT // 2)
            e.tensor_tensor(ev[:, :, :], top_v[:, :, 0:TOPK], top_v[:, :, 0:1].to_broadcast([P, TT, TOPK]), ALU.subtract).then_inc(f_dv, 1)
            link(e.tensor_copy(topi_f[:, :, :], top_i[:, :, 0:TOPK]))
            link(e.tensor_tensor(oh[:, :, :], iota_f[:, None, 0:E].to_broadcast([P, TT * TOPK, E]),
                                 topi_f[:, :, :].rearrange("p t k -> p (t k)")[:, :, None].to_broadcast([P, TT * TOPK, E]), ALU.is_equal))
            oh4 = oh[:, :, :].rearrange("p (t k) e -> p t k e", k=TOPK)
            ohg4 = ohg[:, :, :].rearrange("p (t k) e -> p t k e", k=TOPK)
            r3 = [rt[:, i, :].rearrange("p (t e) -> p t e", t=TT) for i in range(5)]
            e.tensor_tensor(r3[0], oh4[:, :, 0, :], oh4[:, :, 1, :], ALU.add)
            link(e.tensor_tensor(r3[1], oh4[:, :, 2, :], oh4[:, :, 3, :], ALU.add))
            link(e.tensor_tensor(r3[2], r3[0], r3[1], ALU.add))
            e.tensor_copy(routed_bf[:, :], rt[:, 2, :]).then_inc(f_bf, 1)
            link(e.memset(before[:, 0, :], 0.0))
            e.wait_ge(f_pe, 2)
            for t in range(TT):
                link(e.tensor_tensor(before[:, t + 1, :], bank[1][:, E * t:E * t + E], before[:, t, :], ALU.add))
            count = before[:, TT, :]
            link(e.tensor_scalar(npass[:, :], count, 0.0, None, ALU.is_gt))
            for i in range(1, S // SLOTS):
                link(e.scalar_tensor_tensor(out=npass[:, :], in0=count, scalar=float(SLOTS * i), in1=npass[:, :], op0=ALU.is_gt, op1=ALU.add))
            link(e.memset(scan[:, :, :], 0.0))
            link(e.tensor_copy(scan[:, 0, 16:], npass[:, :]))
            cur = 0
            for d in (1, 2, 4, 8, 16):
                link(e.tensor_tensor(scan[:, 1 - cur, 16:], scan[:, cur, 16:], scan[:, cur, 16 - d:16 + E - d], ALU.add))
                cur = 1 - cur
            pinc = scan[:, cur, 16:]
            link(e.tensor_tensor(pexc[:, :], pinc, npass[:, :], ALU.subtract))
            link(e.tensor_scalar(pexc[:, :], pexc[:, :], float(SLOTS), None, ALU.mult))
            pid, expert, left, has_b = (pass_c[:, i:i + 1] for i in range(4))
            link(e.tensor_scalar(pid, dum[:, 0:1], float(-DUMMY), None, ALU.add))
            link(e.tensor_scalar(pass_e[:, 0, :], pinc, pid, None, ALU.is_le))
            link(e.tensor_reduce(expert, pass_e[:, 0, :], AX.X, ALU.add))
            link(e.tensor_scalar(pass_e[:, 1, :], iota_f[:, 0:E], expert, None, ALU.is_equal))
            link(e.tensor_tensor(pass_e[:, 2, :], count, pexc[:, :], ALU.add))
            link(e.tensor_tensor(pass_e[:, 3, :], pass_e[:, 1, :], pass_e[:, 2, :], ALU.mult))
            link(e.tensor_reduce(left, pass_e[:, 3, :], AX.X, ALU.add))
            link(e.scalar_tensor_tensor(out=left, in0=pid, scalar=float(-SLOTS), in1=left, op0=ALU.mult, op1=ALU.add))
            e.tensor_scalar(has_b, left, float(P), None, ALU.is_gt).then_inc(f_col, 1)
            e.tensor_scalar(b_bf[:, :], left, float(P), None, ALU.is_gt).then_inc(f_col, 1)
            e.wait_ge(f_row, 3)
            link(e.tensor_copy(b_row[:, :], bank[2][0:1, P:P + NT]))
            link(e.tensor_scalar(table[:, 0:NT], bank[2][0:1, 0:NT], float(E - 1), None, ALU.min))
            link(e.tensor_copy(table[:, NT:2 * NT], b_row[:, :]))
            link(e.tensor_tensor(table[:, 2 * NT:3 * NT], bank[2][0:1, 2 * P:2 * P + NT], b_row[:, :], ALU.subtract))
            link(e.tensor_copy(table[:, 3 * NT:], pinc[0:1, E - 1:E]))
            e.sem_inc(table_ok, 1)
            link(e.tensor_tensor(r3[0], bank[0][:, 0:TT * E].rearrange("p (t e) -> p t e", t=TT), before[:, 0:TT, :], ALU.add))
            link(e.tensor_tensor(r3[1], r3[0], pexc[:, None, :].to_broadcast([P, TT, E]), ALU.add))
            link(e.tensor_tensor(r3[4], r3[1], r3[2], ALU.mult))
            link(e.tensor_scalar(slot_of[:, :, :], r3[4], -1.0, None, ALU.add))
            e.wait_ge(f_exp, 1)
            link(e.tensor_reduce(esum[:, :], ev[:, :, :], AX.X, ALU.add))
            link(e.reciprocal(esum[:, :], esum[:, :]))
            link(e.tensor_tensor(gk[:, :, :], ev[:, :, :], esum[:, :, None].to_broadcast([P, TT, TOPK]), ALU.mult))
            link(e.tensor_tensor(ohg[:, :, :], oh[:, :, :],
                                 gk[:, :, :].rearrange("p t k -> p (t k)")[:, :, None].to_broadcast([P, TT * TOPK, E]), ALU.mult))
            e.tensor_tensor(r3[0], ohg4[:, :, 0, :], ohg4[:, :, 1, :], ALU.add)
            link(e.tensor_tensor(r3[1], ohg4[:, :, 2, :], ohg4[:, :, 3, :], ALU.add))
            link(e.tensor_tensor(r3[3], r3[0], r3[1], ALU.add))
            link(e.tensor_copy(rows_bf[:, :, :, 3], r3[3]))
            link(e.tensor_tensor(r3[0], r3[3], rows_bf[:, :, :, 3], ALU.subtract))
            link(e.tensor_copy(rows_bf[:, :, :, 4], r3[0]))
            link(e.tensor_tensor(rows_bf[:, :, :, 5], r3[0], rows_bf[:, :, :, 4], ALU.subtract))
            e.sem_inc(f_done, 1)

            n_pass = e.value_load(table[0:1, 3 * NT:3 * NT + 1], min_val=1, max_val=MAX_PASSES)

            def row_numbers(n):
                e.wait_ge(g_imm, 1 + n + 1)
                k = 4 * n
                e.tensor_copy(islot[:, :], bank[4][:, 0:12]).then_inc(g_ich, 1)
                e.wait_ge(g_ich, 1 + k + 1)
                i6 = islot[:, :].rearrange("p (b c) -> p b c", b=2)
                e.tensor_tensor(itmp[:, 0, :], i6[:, :, 0], i6[:, :, 1], ALU.add)
                e.tensor_tensor(gsum[:, :], i6[:, :, 3], i6[:, :, 4], ALU.add)
                e.tensor_tensor(itmp[:, 1, :], i6[:, :, 2], dum[:, :], ALU.mult).then_inc(g_ich, 1)
                e.wait_ge(g_ich, 1 + k + 2)
                e.tensor_tensor(itmp[:, 2, :], dum[:, :], itmp[:, 1, :], ALU.subtract).then_inc(g_ich, 1)
                e.wait_ge(g_ich, 1 + k + 3)
                e.tensor_tensor(idx_next[:, :], itmp[:, 0, :], itmp[:, 2, :], ALU.add).then_inc(g_idx, 1)
                e.tensor_tensor(gate_next[:, :], gsum[:, :], i6[:, :, 5], ALU.add).then_inc(g_idx, 1)
                e.sem_inc(g_ich, 1)

            def rest_of_weights(c):
                e.tensor_tensor(w_lo[:, c % SPLIT, :], ring[:, c % NSLOT, :], w_hi[:, c % SPLIT, :].bitcast(F32), ALU.subtract).then_inc(g_lo, 1)

            def rest_of_rows(b, at):
                e.wait_ge(g_xhi[b], 1 + 2 * at + 2)
                for i in range(2):
                    e.tensor_tensor(xT[b][1][:, 4 * i:4 * i + 4, :], bank[4 + i][:, :].rearrange("p (k t) -> p k t", k=4),
                                    xT[b][0][:, 4 * i:4 * i + 4, :].bitcast(F32), ALU.subtract).then_inc(g_xev[b], 1)

            def pick_tokens(ex, n, first):
                e.wait_ge(g_imm, 1 + n)
                if first:
                    e.memset(base[:, :], 0.0).then_inc(g_base, 1)
                else:
                    e.tensor_scalar(base[:, :], base[:, :], float(-SLOTS), None, ALU.add).then_inc(g_base, 1)
                e.wait_ge(g_base, 1 + n + 1)
                e.tensor_scalar(slot_col[:, :, :], slot_of[:, :, bass.ds(ex, 1)], base[:, 0:1], None, ALU.add).then_inc(g_col, 1)
                e.wait_ge(g_col, 1 + n + 1)
                for t in range(TT):
                    e.tensor_scalar(pick[:, t, :], iota_bf[:, :], slot_col[:, t, :], None, ALU.is_equal).then_inc(g_pick, 1)

            ex0 = e.value_load(table[0:1, 0:1], min_val=0, max_val=E - 1)
            pick_tokens(ex0, 0, True)
            row_numbers(0)
            for c in range(SPLIT):
                e.wait_ge(g_hi, 1 + c + 1)
                rest_of_weights(c)
            rest_of_rows(0, 0)
            hb0 = e.value_load(table[0:1, NT:NT + 1], min_val=0, max_val=1)
            with e.If(hb0 > 0):
                rest_of_rows(1, 0)
            with e.Fori(0, n_pass) as p:
                hb = e.value_load(table[0:1, bass.ds(p + NT, 1)], min_val=0, max_val=1)
                nb = e.value_load(table[0:1, bass.ds(p + 2 * NT, 1)], min_val=0, max_val=MAX_PASSES)
                exn = e.value_load(table[0:1, bass.ds(p + 1, 1)], min_val=0, max_val=E - 1)
                hbn = e.value_load(table[0:1, bass.ds(p + 1 + NT, 1)], min_val=0, max_val=1)

                def add_bias(b, s, at):
                    e.wait_ge(g_half[b], 1 + HALVES * at + 2 * s + 2)
                    if s == 0:
                        e.wait_ge(g_bgu, 1 + p + 1)
                    e.wait_ge(g_act[b], 1 + 4 * at + s)
                    e.tensor_tensor(gu[b][:, :], bank[2 * b + s % 2][:, :], bbc[:, 2 * FQ * s:2 * FQ * s + 2 * FQ], ALU.add).then_inc(g_add[b], 1)
                    e.wait_ge(g_add[b], 2 + ADDS * at + s + 1)
                    e.tensor_scalar(gu[b][:, 0:FQ], gu[b][:, 0:FQ], LIMIT, None, ALU.min).then_inc(g_clip[b], 1)
                    e.tensor_scalar(gu[b][:, FQ:2 * FQ], gu[b][:, FQ:2 * FQ], LIMIT, -LIMIT, ALU.min, ALU.max).then_inc(g_clip[b], 1)

                def add_down_bias(b, h, at):
                    e.wait_ge(g_half[b], 1 + HALVES * at + 12 + h)
                    if h == 0:
                        e.wait_ge(g_bd, 1 + p + 1)
                        e.wait_ge(g_added, p + 1)
                    e.tensor_tensor(ys[b][:, 512 * h:512 * h + 512], bank[2 * b + h][:, :], bbc[:, 2 * D + 512 * h:2 * D + 512 * h + 512], ALU.add).then_inc(g_add[b], 1)

                def swiglu(b, s, at):
                    e.wait_ge(g_sig[b], 1 + 4 * at + s + 1)
                    e.tensor_tensor(sg[b][:, :], gu[b][:, 0:FQ], sg[b][:, :], ALU.mult).then_inc(g_m1[b], 1)
                    e.wait_ge(g_m1[b], 1 + 4 * at + s + 1)
                    e.wait_ge(g_clip[b], 1 + 8 * at + 2 * s + 2)
                    e.wait_ge(g_atr[b], 1 + 4 * at + s)
                    e.scalar_tensor_tensor(out=act[b][:, :], in0=gu[b][:, FQ:2 * FQ], scalar=1.0, in1=sg[b][:, :],
                                           op0=ALU.add, op1=ALU.mult).then_inc(g_act[b], 1)

                def rest_of_act(b, s, at):
                    e.wait_ge(g_aev[b], 1 + 4 * at + s + 1)
                    e.tensor_tensor(aT[b][1][:, 2 * s:2 * s + 2, :], bank[6 + b][:, 0:FQ].rearrange("p (k t) -> p k t", k=2),
                                    aT[b][0][:, 2 * s:2 * s + 2, :].bitcast(F32), ALU.subtract).then_inc(g_alo[b], 1)

                def weights(c):
                    if c < 12 and c not in POOL_LO:
                        e.wait_ge(g_hi, 1 + 12 * p + c + 1)
                        rest_of_weights(c)
                    elif c >= 12:
                        with e.If(p + 1 < n_pass):
                            e.wait_ge(g_hi, 1 + 12 * p + c + 1)
                            rest_of_weights(c - 12)

                for s in range(STEPS):
                    if s < 4:
                        add_bias(0, s, p)
                        with e.If(hb > 0):
                            add_bias(1, s, nb)
                    if s == 4:
                        rest_of_rows(0, p + 1)
                    if s == 5:
                        with e.If(hbn > 0):
                            rest_of_rows(1, nb + hb)
                        for h in range(2):
                            add_down_bias(0, h, p)
                            with e.If(hb > 0):
                                add_down_bias(1, h, nb)
                            if h == 0:
                                weights(13)
                    if s == 4:
                        rest_of_act(0, 3, p)
                        with e.If(hb > 0):
                            rest_of_act(1, 3, nb)
                    if s == 2:
                        e.wait_ge(g_added, p + 1)
                        e.tensor_copy(idx_cur[:, :], idx_next[:, :])
                        e.tensor_copy(gate_cur[:, :], gate_next[:, :]).then_inc(g_cur, 1)
                        e.wait_ge(g_cur, 1 + p + 1)
                        row_numbers(p + 1)
                    weights(2 * s + 4)
                    if s < 4:
                        swiglu(0, s, p)
                        with e.If(hb > 0):
                            swiglu(1, s, nb)
                    if 1 <= s <= 3:
                        rest_of_act(0, s - 1, p)
                        with e.If(hb > 0):
                            rest_of_act(1, s - 1, nb)
                    if s != 4:
                        weights(2 * s + 5)
                    if s == 0:
                        pick_tokens(exn, p + 1, False)

        @block.tensor
        def _(e):
            for s in (*g_half, *g_atr, *g_xtr, g_imm):
                e.sem_inc(s, 1)
            e.wait_ge(made, 1)

            def x_transpose(t):
                e.wait_ge(xnorm, t + 1)
                if t >= 2:
                    e.wait_ge(xev, 2 * (t - 1))
                for k in range(KT):
                    i = e.transpose(bank[4 + 2 * (t % 2) + k // 4][:, P * (k % 4):P * (k % 4) + P], xt[t % 2][:, P * k:P * k + P], ident[:, :])
                i.then_inc(xtr, 1)
            for t in range(TT):
                x_transpose(t)

            def q_transpose(n):
                e.wait_ge(qnorm, n + 1)
                if n >= 2:
                    e.wait_ge(qev, q_evacs(n - 1))
                for i in range(4):
                    ins = e.transpose(bank[2 + n % 2][:, P * i:P * i + P], qn[n % 2][:, P * i:P * i + P], ident[:, :])
                ins.then_inc(qtr, 1)
            for g in range(3):
                for t in range(TT):
                    n = TT * g + t
                    if n < TT:
                        e.wait_ge(xev, 2 * t + 2)
                    if n >= 2:
                        if n - 2 < 2 * TT:
                            e.wait_ge(qnorm, n - 1)
                        else:
                            e.wait_ge(vev, n - 2 - 2 * TT + 1)
                    for k in range(KT):
                        if k % 4 == 0:
                            wait_item(e, 2 * g + k // 4)
                        ins = e.matmul(bank[n % 2][:, :], hT[:, k, P * t:P * t + P], item_view(2 * g + k // 4, 0, 4, 512)[:, k % 4, :],
                                       start=(k == 0), stop=(k == KT - 1))
                    ins.then_inc(proj, 1)
                    if 1 <= n <= 2 * TT:
                        q_transpose(n - 1)
                e.wait_ge(proj, TT * (g + 1))
                e.sem_inc(w_used, 2)

            def scores(n):
                h, rb, cb, v = unit(n)
                if n < 2:
                    e.wait_ge(qev, q_evacs(2 * TT))
                else:
                    e.wait_ge(smin, n - 1)
                h0 = HD * (h % 2)
                kg = qkT[h0:h0 + HD, h // 2, :].rearrange("p (r c) -> p r c", c=GRID_W)
                q0 = 512 * rb + P * cb
                e.matmul(bank[2 + n % 2][:, 0:KEYS].rearrange("p (r c) -> p r c", c=KC),
                         qkT[h0:h0 + HD, 4 + h // 2, q0:q0 + P],
                         kg[:, ROW_BASE[rb]:ROW_BASE[rb] + KR, COL_BASE[cb]:COL_BASE[cb] + KC], start=True, stop=True).then_inc(sc, 1)

            def prob_transpose(n):
                e.wait_ge(snorm, n + 1)
                if n >= 2:
                    e.wait_ge(pev, n - 1)
                for i in range(3):
                    ins = e.transpose(bank[4 + n % 2][:, P * i:P * i + P], prob[n % 2][:, P * i:P * i + P], ident[:, :])
                ins.then_inc(ptr, 1)

            def weighted(n):
                h, rb, cb, v = unit(n)
                e.wait_ge(pev, n + 1)
                if n == 0:
                    e.wait_ge(v_moved, 256)
                if n >= 2:
                    e.wait_ge(oev, n - 1)
                h0 = HD * (h % 2)
                for i in range(3):
                    ins = e.matmul(bank[6 + n % 2][h0:h0 + HD, 0:P], vb[:, cb, rb + i, HD * h:HD * h + HD],
                                   probT[n % 2][:, P * i:P * i + P], start=(i == 0), stop=(i == 2))
                ins.then_inc(pvd, 1)
            un = 0
            for m in range(24):
                j, part, hf = m // 6, (m % 6) // 2, m % 2
                it = IT_CONV + 2 * j + (part == 2)
                wait_item(e, it)
                wv = item_view(it, 1024 if part == 1 else 0, 8, P)
                if m < 2:
                    e.wait_ge(vev, TT - 1 + m)
                else:
                    jj, pp, hh = (m - 2) // 6, ((m - 2) % 6) // 2, (m - 2) % 2
                    e.wait_ge((uev, cmul, bmul)[pp], 2 * jj + hh + 1)
                for k in range(KT):
                    ins = e.matmul(bank[m % 2][:, :], wv[:, k, :], hT[:, k, 512 * hf:512 * hf + 512], start=(k == 0), stop=(k == KT - 1))
                ins.then_inc(proj, 1)
                if (part, hf) in ((1, 1), (2, 1)):
                    e.wait_ge(proj, 3 * TT + m + 1)
                    e.sem_inc(w_used, 1)
                while un < unit_end[m]:
                    scores(un)
                    if un >= 1:
                        prob_transpose(un - 1)
                    if un >= 2:
                        weighted(un - 2)
                    un += 1
            prob_transpose(units - 1)
            weighted(units - 2)
            weighted(units - 1)

            for n in range(16):
                d, hf = n // 2, n % 2
                cols = slice(512 * hf, 512 * hf + 512)
                b0 = 4 * (n % 2)
                if n == 0:
                    e.wait_ge(bmul, 8)
                    e.wait_ge(smin, units)
                elif n == 1:
                    e.wait_ge(pev, units)
                    e.wait_ge(oev, units)
                else:
                    e.wait_ge(mmul, 2 * (n - 1))
                wait_item(e, IT_MERGE + 2 * d + 1)
                if n == 0:
                    e.wait_ge(oev, units)
                for g, src in enumerate((ypre, oT)):
                    for k in range(4):
                        ins = e.matmul(bank[b0 + 2 + g][:, :], item_view(IT_MERGE + 2 * d + 1, 512 * g, 4, P)[:, k, :], src[:, k, cols],
                                       start=(k == 0), stop=(k == 3))
                    ins.then_inc(mtile, 1)
                e.wait_ge(gate_lo_ok, d + 1)
                for g in range(2):
                    for k in range(KT):
                        if n == 0 and g == 0:
                            e.wait_ge(h_lo_ok, k + 1)
                        at = 1024 * g + P * k
                        w_up, w_rest = gate_hi[:, at:at + P], ring_lo[:, (IT_MERGE + 2 * d) % MSLOT, at:at + P]
                        e.matmul(bank[b0 + g][:, :], w_up, h_hi[:, k, cols], start=(k == 0), stop=False)
                        e.matmul(bank[b0 + g][:, :], w_up, h_lo[:, k, cols], start=False, stop=False)
                        ins = e.matmul(bank[b0 + g][:, :], w_rest, h_hi[:, k, cols], start=False, stop=(k == KT - 1))
                    ins.then_inc(mtile, 1)
                if hf == 1:
                    e.wait_ge(mtile, 4 * n + 4)
                    e.sem_inc(w_used, 2)

            def h2_transpose(t):
                e.wait_ge(e_xn, t + 1)
                if t:
                    e.wait_ge(e_ht, 2 * t)
                for k in range(KT):
                    ins = e.transpose(bank[4 + k // 4][:, P * (k % 4):P * (k % 4) + P], xn[t % 2][:, P * k:P * k + P], ident[:, :])
                ins.then_inc(e_tr, 1)

            def router(t):
                e.wait_ge(e_ht, 2 * t + 2)
                if t >= 2:
                    e.wait_ge(e_lc, t - 1)
                dst = bank[6 + t % 2][:, 0:E]
                for k in range(KT):
                    e.matmul(dst, h2T[t % 2][:, k, :], wr[:, k, :], start=(k == 0), stop=False)
                e.matmul(dst, ones_row[0:1, :], br_row[0:1, :], start=False, stop=True).then_inc(e_lg, 1)
            for t in range(TT):
                if t == 0:
                    e.wait_ge(mixd, 16)
                if t >= 2:
                    e.wait_ge(e_x1, 2 * (t - 1))
                for i in range(2):
                    for k in range(KT):
                        if t == 0 and i == 0 and k % 2 == 0:
                            wait_item(e, IT_WO + k // 2)
                        ins = e.matmul(bank[2 * (t % 2) + i][:, :], mixedT[:, k, P * t:P * t + P],
                                       item_view(IT_WO + k // 2, 0, 2, D)[:, k % 2, 512 * i:512 * i + 512], start=(k == 0), stop=(k == KT - 1))
                    ins.then_inc(e_mm, 1)
                if t:
                    h2_transpose(t - 1)
                if t >= 2:
                    router(t - 2)
            e.wait_ge(e_mm, 2 * TT)
            e.sem_inc(w_used, 4)
            h2_transpose(TT - 1)
            router(TT - 2)
            router(TT - 1)

            e.wait_ge(f_bf, 1)
            e.wait_ge(e_x1, 2 * TT)
            e.matmul(bank[0][:, 0:TT * E], tri_bf[:, :], routed_bf[:, :], start=True, stop=True).then_inc(f_pe, 1)
            e.matmul(bank[1][:, 0:TT * E], ones_bf[:, :], routed_bf[:, :], start=True, stop=True).then_inc(f_pe, 1)

            e.wait_ge(f_col, 2)
            e.matmul(bank[2][0:1, 0:P], pass_c[:, 1:2], ident[:, :], start=True, stop=True).then_inc(f_row, 1)
            e.matmul(bank[2][0:1, P:2 * P], pass_c[:, 3:4], ident[:, :], start=True, stop=True).then_inc(f_row, 1)
            e.matmul(bank[2][0:1, 2 * P:3 * P], b_bf[:, :], tri_bf[:, :], start=True, stop=True).then_inc(f_row, 1)

            e.wait_ge(table_ok, 1)
            n_pass = e.value_load(table[0:1, 3 * NT:3 * NT + 1], min_val=1, max_val=MAX_PASSES)

            def slot_rows(ex, n):
                e.wait_ge(g_pick, 1 + TT * n + TT)
                for b in range(2):
                    for t in range(TT):
                        ins = e.matmul(bank[4][:, 6 * b:6 * b + 6], pick[:, t, P * b:P * b + P],
                                       rows_bf[:, t, bass.ds(ex, 1), :].rearrange("p e c -> p (e c)"), start=(t == 0), stop=(t == TT - 1))
                ins.then_inc(g_imm, 1)

            def rows_transpose(b, at, n):
                e.wait_ge(g_gat[b], 16 * at + 16)
                for k in range(KT):
                    ins = e.transpose(bank[4 + k // 4][:, P * (k % 4):P * (k % 4) + P], xg[b][:, P * k:P * k + P], ident[:, :])
                ins.then_inc(g_xtr[b], 1)

            ex = e.value_load(table[0:1, 0:1], min_val=0, max_val=E - 1)
            hb = e.value_load(table[0:1, NT:NT + 1], min_val=0, max_val=1)
            slot_rows(ex, 0)
            rows_transpose(0, 0, 0)
            with e.If(hb > 0):
                e.wait_ge(g_xev[0], 1 + 2)
                rows_transpose(1, 0, 0)
            with e.Fori(0, n_pass) as p:
                hb = e.value_load(table[0:1, bass.ds(p + NT, 1)], min_val=0, max_val=1)
                nb = e.value_load(table[0:1, bass.ds(p + 2 * NT, 1)], min_val=0, max_val=MAX_PASSES)
                exn = e.value_load(table[0:1, bass.ds(p + 1, 1)], min_val=0, max_val=E - 1)
                hbn = e.value_load(table[0:1, bass.ds(p + 1 + NT, 1)], min_val=0, max_val=1)

                def product(b, dst, src, k, c, off, start, stop):
                    hi, lo = w_hi[:, c % SPLIT, off:off + 512], w_lo[:, c % SPLIT, off:off + 512]
                    e.matmul(dst, src[0][:, k, :], hi, start=start, stop=False)
                    e.matmul(dst, src[0][:, k, :], lo, start=False, stop=False)
                    return e.matmul(dst, src[1][:, k, :], hi, start=False, stop=stop)

                def products(b, c, at):
                    s = c // 2
                    if b == 0:
                        wait_lo(e.wait_ge, p, c)
                    if c == 0:
                        e.wait_ge(g_xev[b], 1 + 2 * at + 2)
                    if c < 8:
                        if c % 2 == 0:
                            e.wait_ge(g_add[b], 2 + ADDS * at + s - 1)
                        for i in range(4):
                            k = 4 * (c % 2) + i
                            ins = product(b, bank[2 * b + s % 2][:, :], xT[b], k, c, 512 * i, k == 0, k == KT - 1)
                        ins.then_inc(g_half[b], 1)
                    else:
                        e.wait_ge(g_alo[b], 1 + 4 * at + c - 8 + 1)
                        for h in range(2):
                            if c == 8:
                                e.wait_ge(g_add[b], 2 + ADDS * at + 3 + h)
                            for i in range(2):
                                k = 2 * (c - 8) + i
                                ins = product(b, bank[2 * b + h][:, :], aT[b], k, c, D * i + 512 * h, k == 0, k == KT - 1)
                            if h == 1 or c == 11:
                                ins.then_inc(g_half[b], 1)

                def act_transpose(b, s, at):
                    e.wait_ge(g_act[b], 1 + 4 * at + s + 1)
                    e.wait_ge(g_alo[b], 1 + 4 * at + s)
                    for k in range(2):
                        ins = e.transpose(bank[6 + b][:, P * k:P * k + P], act[b][:, P * k:P * k + P], ident[:, :])
                    ins.then_inc(g_atr[b], 1)

                for c in range(12):
                    products(0, c, p)
                    with e.If(hb > 0):
                        products(1, c, nb)
                    if c in (4, 6, 8, 9):
                        act_transpose(0, c // 2 - 2 + c % 2, p)
                        with e.If(hb > 0):
                            act_transpose(1, c // 2 - 2 + c % 2, nb)
                    if c == 4:
                        e.wait_ge(g_xev[1], 1 + 2 * (nb + hb))
                        slot_rows(exn, p + 1)
                    if c == 9:
                        rows_transpose(0, p + 1, p + 1)
                    if c == 10:
                        with e.If(hbn > 0):
                            e.wait_ge(g_xev[0], 1 + 2 * p + 4)
                            rows_transpose(1, nb + hb, p + 1)


_INPUTS = ["x", "nmix", "w_in", "convw", "w_oc", "qkgain", "windows", "w_oa", "w_o", "nffn", "w_r", "b_r",
           "w_gate", "b_gate", "w_up", "b_up", "w_down", "b_down"]


def kernel(**inputs):
    import concourse.bacc as _bacc
    import ml_dtypes
    from concourse.bass_utils import run_bass_kernel_spmd as _run

    arrays = {n: np.ascontiguousarray(a) for n, a in layout(inputs).items()}
    arrays["masks"] = window_masks().astype(ml_dtypes.bfloat16)
    nc = _bacc.Bacc("TRN2", target_bir_lowering=False, num_devices=1)
    aps = {n: nc.dram_tensor(f"in_{n}", arrays[n].shape, mybir.dt.from_np(arrays[n].dtype), kind="ExternalInput").ap()
           for n in _INPUTS + ["masks"]}
    out = nc.dram_tensor("out_rows", [ROWS_OUT, D], F32, kind="ExternalOutput").ap()
    build(nc, aps, out)
    r = _run(nc, [{f"in_{n}": arrays[n] for n in _INPUTS + ["masks"]}], core_ids=[0])
    return r.results[0]["out_rows"][:S].reshape(1, S, D)
```
